# Optimizing a Trainium2 kernel written in Bass

```python
import jax, jax.numpy as jnp
from jax import lax
import numpy as np

D_MODEL = 1024
BATCH = 1
SEQ = 1024
DEPTH = 1

MEM_LEN = 256
HEAD_DIM = 64
EPS = 1e-6
N_LRU_HEADS = 6
D_LRU = N_LRU_HEADS * HEAD_DIM
CONV_WIDTH = 4
LRU_C = 8.0
N_SWA_HEADS = 6
N_SWA_KV = 2
SWA_GROUP = N_SWA_HEADS // N_SWA_KV
D_SWA = N_SWA_HEADS * HEAD_DIM
D_SWA_KV = N_SWA_KV * HEAD_DIM
WINDOW = 128
BLOCK = 128
N_MEM_HEADS = 4
D_MEM = N_MEM_HEADS * HEAD_DIM
D_MIX = D_LRU + D_SWA + D_MEM
D_IN = 2 * D_LRU + D_SWA + 2 * D_SWA_KV + D_MEM
N_EXPERTS = 32
TOP_K = 4
D_FF = D_MODEL
SWIGLU_ALPHA = 1.702
SWIGLU_LIMIT = 7.0
MOE_BLOCK = 128

kernel_name = "hymba_style_rglru_swa_sink_mem_moe"

def rms_norm(x, g):
    xf = x.astype(jnp.float32)
    y = xf * lax.rsqrt(jnp.mean(xf * xf, axis=-1, keepdims=True) + EPS)
    return (y * g.astype(jnp.float32)).astype(x.dtype)

def causal_depthwise_conv(x, w, b):
    S = x.shape[1]
    xp = jnp.pad(x, ((0, 0), (CONV_WIDTH - 1, 0), (0, 0)))
    out = b + xp[:, 0:S] * w[0]
    for k in range(1, CONV_WIDTH):
        out = out + xp[:, k:k + S] * w[k]
    return out

def rg_lru(xb, w_a, b_a, w_x, b_x, lam):
    B, S, _ = xb.shape
    xf = xb.astype(jnp.float32)
    xh = xf.reshape(B, S, N_LRU_HEADS, HEAD_DIM)
    r = jax.nn.sigmoid(jnp.einsum('bshi,hij->bshj', xh, w_a.astype(jnp.float32)).reshape(B, S, D_LRU) + b_a)
    i = jax.nn.sigmoid(jnp.einsum('bshi,hij->bshj', xh, w_x.astype(jnp.float32)).reshape(B, S, D_LRU) + b_x)
    log_a = -LRU_C * r * jax.nn.softplus(-lam.astype(jnp.float32))
    a = jnp.exp(log_a)
    bx = jnp.sqrt(-jnp.expm1(2.0 * log_a)) * (i * xf)

    def combine(left, right):
        a_l, b_l = left
        a_r, b_r = right
        return a_l * a_r, a_r * b_l + b_r

    _, h = lax.associative_scan(combine, (a, bx), axis=1)
    return h.astype(xb.dtype)

def sliding_window_sink_attention(q, k, v, sinks):
    B, S, _, _ = q.shape
    NB = S // BLOCK
    scale = HEAD_DIM ** -0.5
    qb = q.reshape(B, NB, BLOCK, N_SWA_KV, SWA_GROUP, HEAD_DIM)
    kb = k.reshape(B, NB, BLOCK, N_SWA_KV, HEAD_DIM)
    vb = v.reshape(B, NB, BLOCK, N_SWA_KV, HEAD_DIM)
    pad = ((0, 0), (1, 0), (0, 0), (0, 0), (0, 0))
    kk = jnp.concatenate([jnp.pad(kb, pad)[:, :-1], kb], axis=2)
    vv = jnp.concatenate([jnp.pad(vb, pad)[:, :-1], vb], axis=2)
    s = jnp.einsum('bnqhgd,bnkhd->bnhgqk', qb, kk).astype(jnp.float32) * scale
    qi = jnp.arange(BLOCK)[:, None]
    kj = jnp.arange(2 * BLOCK)[None, :]
    rel = qi + BLOCK - kj
    band = (rel >= 0) & (rel < WINDOW)
    has_prev = (jnp.arange(NB)[:, None] > 0) | (kj >= BLOCK)
    mask = band[None] & has_prev[:, None, :]
    s = jnp.where(mask[None, :, None, None], s, -jnp.inf)
    sink = jnp.broadcast_to(sinks.astype(jnp.float32).reshape(N_SWA_KV, SWA_GROUP)[None, None, :, :, None, None],
                            s.shape[:-1] + (1,))
    p = jax.nn.softmax(jnp.concatenate([s, sink], axis=-1), axis=-1)[..., :-1]
    o = jnp.einsum('bnhgqk,bnkhd->bnqhgd', p.astype(v.dtype), vv)
    return o.reshape(B, S, D_SWA)

def memory_cross_attention(q, km, vm):
    B, S, _, _ = q.shape
    s = jnp.einsum('bshd,bmhd->bhsm', q, km).astype(jnp.float32) * (HEAD_DIM ** -0.5)
    p = jax.nn.softmax(s, axis=-1)
    o = jnp.einsum('bhsm,bmhd->bshd', p.astype(vm.dtype), vm)
    return o.reshape(B, S, D_MEM)

def clamped_swiglu(h):
    x_glu = jnp.minimum(h[..., ::2], SWIGLU_LIMIT)
    x_lin = jnp.clip(h[..., 1::2], -SWIGLU_LIMIT, SWIGLU_LIMIT)
    return x_glu * jax.nn.sigmoid(SWIGLU_ALPHA * x_glu) * (x_lin + 1.0)

def moe(xn, w_router, b_router, w1, b1, w2, b2):
    Bn, S, D = xn.shape
    N = Bn * S
    xt = xn.reshape(N, D)
    logits = (xt @ w_router).astype(jnp.float32) + b_router.astype(jnp.float32)
    top_vals, top_idx = lax.top_k(logits, TOP_K)
    gates = jax.nn.softmax(top_vals, axis=-1)
    A = N * TOP_K
    e_flat = top_idx.reshape(A).astype(jnp.int32)
    g_flat = gates.reshape(A)
    tok_flat = jnp.repeat(jnp.arange(N, dtype=jnp.int32), TOP_K)
    order = jnp.argsort(e_flat)
    e_sorted = e_flat[order]
    counts = jnp.bincount(e_flat, length=N_EXPERTS)
    starts = jnp.cumsum(counts) - counts
    padded = ((counts + MOE_BLOCK - 1) // MOE_BLOCK) * MOE_BLOCK
    pad_ends = jnp.cumsum(padded)
    pad_starts = pad_ends - padded
    dest = pad_starts[e_sorted] + jnp.arange(A, dtype=jnp.int32) - starts[e_sorted]
    n_blocks = -(-A // MOE_BLOCK) + N_EXPERTS
    P = n_blocks * MOE_BLOCK
    tok_buf = jnp.zeros((P,), jnp.int32).at[dest].set(tok_flat[order])
    gate_buf = jnp.zeros((P,), jnp.float32).at[dest].set(g_flat[order])
    block_expert = jnp.minimum(
        jnp.searchsorted(pad_ends, jnp.arange(n_blocks) * MOE_BLOCK, side='right'), N_EXPERTS - 1)
    xb = xt[tok_buf].reshape(n_blocks, MOE_BLOCK, D)

    def expert_block(args):
        xblk, e = args
        h = xblk @ w1[e] + b1[e]
        return clamped_swiglu(h) @ w2[e] + b2[e]

    yb = lax.map(expert_block, (xb, block_expert)).reshape(P, D)
    out = jnp.zeros((N, D), jnp.float32).at[tok_buf].add(yb.astype(jnp.float32) * gate_buf[:, None])
    return out.astype(xn.dtype).reshape(Bn, S, D)

def setup_inputs(seed: int = 0) -> dict:
    key = jax.random.key(seed)
    ks = jax.random.split(key, 32)
    f32 = jnp.float32
    L = DEPTH

    def nrm(k, shape, scale):
        return jax.random.normal(k, shape, f32) * scale

    def gain(k, shape):
        return 1.0 + 0.05 * jax.random.normal(k, shape, f32)

    u = jax.random.uniform(ks[8], (L, D_LRU), f32, 0.9, 0.999)
    a0 = u ** (1.0 / LRU_C)
    lam = jnp.log(a0) - jnp.log1p(-a0)
    return {
        "x": jax.random.normal(ks[0], (BATCH, SEQ, D_MODEL), f32),
        "mem": jax.random.normal(ks[1], (BATCH, MEM_LEN, D_MODEL), f32),
        "g_mix": gain(ks[2], (L, D_MODEL)),
        "w_in": nrm(ks[3], (L, D_MODEL, D_IN), D_MODEL ** -0.5),
        "conv_w": nrm(ks[4], (L, CONV_WIDTH, D_LRU), CONV_WIDTH ** -0.5),
        "conv_b": nrm(ks[5], (L, D_LRU), 0.02),
        "lru_wa": nrm(ks[6], (L, N_LRU_HEADS, HEAD_DIM, HEAD_DIM), HEAD_DIM ** -0.5),
        "lru_ba": nrm(ks[7], (L, D_LRU), 0.02),
        "lru_wx": nrm(ks[9], (L, N_LRU_HEADS, HEAD_DIM, HEAD_DIM), HEAD_DIM ** -0.5),
        "lru_bx": nrm(ks[10], (L, D_LRU), 0.02),
        "lru_lambda": lam,
        "q_norm_swa": gain(ks[11], (L, HEAD_DIM)),
        "k_norm_swa": gain(ks[12], (L, HEAD_DIM)),
        "swa_sinks": nrm(ks[13], (L, N_SWA_HEADS), 0.5),
        "g_mem": gain(ks[14], (L, D_MODEL)),
        "w_mem_kv": nrm(ks[15], (L, D_MODEL, 2 * D_MEM), D_MODEL ** -0.5),
        "q_norm_mem": gain(ks[16], (L, HEAD_DIM)),
        "k_norm_mem": gain(ks[17], (L, HEAD_DIM)),
        "g_out_lru": gain(ks[18], (L, D_LRU)),
        "g_out_swa": gain(ks[19], (L, D_SWA)),
        "g_out_mem": gain(ks[20], (L, D_MEM)),
        "w_out": nrm(ks[21], (L, D_MIX, D_MODEL), D_MIX ** -0.5),
        "g_ffn": gain(ks[22], (L, D_MODEL)),
        "w_router": nrm(ks[23], (L, D_MODEL, N_EXPERTS), D_MODEL ** -0.5),
        "b_router": nrm(ks[24], (L, N_EXPERTS), 0.01),
        "w1": nrm(ks[25], (L, N_EXPERTS, D_MODEL, 2 * D_FF), D_MODEL ** -0.5),
        "b1": nrm(ks[26], (L, N_EXPERTS, 2 * D_FF), 0.02),
        "w2": nrm(ks[27], (L, N_EXPERTS, D_FF, D_MODEL), D_FF ** -0.5),
        "b2": nrm(ks[28], (L, N_EXPERTS, D_MODEL), 0.02),
    }

def reference(x, mem, g_mix, w_in, conv_w, conv_b, lru_wa, lru_ba, lru_wx, lru_bx, lru_lambda,
              q_norm_swa, k_norm_swa, swa_sinks, g_mem, w_mem_kv, q_norm_mem, k_norm_mem,
              g_out_lru, g_out_swa, g_out_mem, w_out, g_ffn, w_router, b_router, w1, b1, w2, b2):
    B, S, _ = x.shape
    h = x
    split_at = [D_LRU, 2 * D_LRU, 2 * D_LRU + D_SWA, 2 * D_LRU + D_SWA + D_SWA_KV,
                2 * D_LRU + D_SWA + 2 * D_SWA_KV]
    for l in range(DEPTH):
        xn = rms_norm(h, g_mix[l])
        u = xn @ w_in[l]
        u_lru, u_gate, u_q, u_k, u_v, u_qm = jnp.split(u, split_at, axis=-1)

        xc = causal_depthwise_conv(u_lru, conv_w[l], conv_b[l])
        y_lru = rg_lru(xc, lru_wa[l], lru_ba[l], lru_wx[l], lru_bx[l], lru_lambda[l]) * jax.nn.gelu(u_gate)

        q = rms_norm(u_q.reshape(B, S, N_SWA_HEADS, HEAD_DIM), q_norm_swa[l])
        k = rms_norm(u_k.reshape(B, S, N_SWA_KV, HEAD_DIM), k_norm_swa[l])
        v = u_v.reshape(B, S, N_SWA_KV, HEAD_DIM)
        y_swa = sliding_window_sink_attention(q, k, v, swa_sinks[l])

        mkv = rms_norm(mem, g_mem[l]) @ w_mem_kv[l]
        km = rms_norm(mkv[..., :D_MEM].reshape(B, MEM_LEN, N_MEM_HEADS, HEAD_DIM), k_norm_mem[l])
        vm = mkv[..., D_MEM:].reshape(B, MEM_LEN, N_MEM_HEADS, HEAD_DIM)
        qm = rms_norm(u_qm.reshape(B, S, N_MEM_HEADS, HEAD_DIM), q_norm_mem[l])
        y_mem = memory_cross_attention(qm, km, vm)

        y = jnp.concatenate([rms_norm(y_lru, g_out_lru[l]),
                             rms_norm(y_swa, g_out_swa[l]),
                             rms_norm(y_mem, g_out_mem[l])], axis=-1)
        h = h + y @ w_out[l]

        h = h + moe(rms_norm(h, g_ffn[l]), w_router[l], b_router[l], w1[l], b1[l], w2[l], b2[l])
    return h


_drawn_inputs = setup_inputs


def setup_inputs(seed=0):
    import zlib

    import numpy as np

    out = dict(_drawn_inputs(seed))
    spreads = {}
    factors = {'lru_ba': 6.807, 'lru_bx': 3.945, 'swa_sinks': 6.046, 'b1': 6.773, 'b2': 7.801}
    for name, (base, spread) in spreads.items():
        noise = np.random.default_rng([zlib.crc32(name.encode()), seed]).standard_normal(out[name].shape)
        drawn = base * np.exp(spread * noise) if base else spread * noise
        out[name] = __import__('jax').numpy.asarray(drawn.astype(out[name].dtype))
    for name, factor in factors.items():
        out[name] = (out[name] * factor).astype(out[name].dtype)
    return out
```

```python
from contextlib import ExitStack

import concourse.bass as bass
from concourse import mybir

F32 = mybir.dt.float32
F16 = mybir.dt.float16
BF16 = mybir.dt.bfloat16
I32 = mybir.dt.int32
U32 = mybir.dt.uint32
ALU = mybir.AluOpType
ACT = mybir.ActivationFunctionType
AX_X = mybir.AxisListType.X

P = 128
D = 1024
S = 1024
NT = S // P
KD = D // P
MEM = 256
DH = 64
NQ = 6
NM = 4
DL = 384
LT = DL // P
E = 32
TOPK = 4
FF = 1024
HALF = 512
EPS = 1e-6
LIMIT = 7.0
ALPHA = 1.702
MAXCH = S // P
NCH = 96
XW = D + E
SLOT = 2048
NSLOT = 12
AHEAD_OOB = 1 << 20

LRU, GATE, Q, K, V, QM = 0, 3, 6, 9, 10, 11
NCT = 13
C_GMIX, C_GMEM, C_CONVW, C_CONVB, C_BA, C_BX, C_LAM, C_QS, C_KS, C_QM, C_KM, C_GOL, C_GOS, C_GOM = (
    0, 8, 16, 28, 31, 34, 37, 40, 41, 42, 43, 44, 47, 50)
NCOL = 52
C_EPS, C_SP8, C_NSP8 = 52, 53, 56
NVEC = 10 + 8
NPOOLC = 10
NRT = 3


def hymba_layer(nc, x, mem, g_mix, w_in, conv_w, conv_b, lru_wa, lru_ba, lru_wx, lru_bx, lru_lambda,
                q_norm_swa, k_norm_swa, swa_sinks, g_mem, w_mem_kv, q_norm_mem, k_norm_mem,
                g_out_lru, g_out_swa, g_out_mem, w_out, g_ffn, w_router, b_router, w1, b1, w2, b2,
                xrows, out):
    with ExitStack() as ctx:
        def sb(name, shape, dt=F32):
            return ctx.enter_context(nc.sbuf_tensor(name, shape, dt))

        def sem(name):
            return ctx.enter_context(nc.semaphore(name))

        ring = sb("ring", [P, NSLOT * SLOT])
        xh = sb("xh", [P, NT, D])
        uT = sb("uT", [P, NCT, S])

        wA = ring[:, 0:6144].rearrange("p (k c) -> p k c", k=KD)
        wB = ring[:, 6144:13312].rearrange("p (k c) -> p k c", k=KD)
        mem_sb = ring[:, 13312:15360].rearrange("p (t d) -> p t d", t=2)
        xnT = ring[:, 8 * SLOT:12 * SLOT].rearrange("p (k t) -> p k t", k=KD)
        w_out_sb = ring[:, 8 * SLOT:12 * SLOT].rearrange("p (k c) -> p k c", k=KD)
        lru_tmp = ring[:, 0:6144].rearrange("p (i t) -> p i t", i=6)
        scores_sb = ring[:, 6144:6144 + 3072].rearrange("p (b h k) -> p b h k", b=2, h=NQ)
        probsT = ring[:, 9216:9216 + 1536].rearrange("p (j q) -> p j q", j=12)
        o_sb = ring[:, 10752:10752 + 768].rearrange("p (b c) -> p b c", b=2)
        o_sq = ring[:, 11520:11520 + 384]
        xs = uT[:, 5:9, :]
        w_mem = uT[:, 9:13, :].rearrange("p a b -> p (a b)").rearrange("p (k c) -> p k c", k=KD)
        ms = uT[:, 3:5, :]
        sqscr = uT[:, 0, :]
        memT_v = uT[:, 1:3, :].rearrange("p a b -> p (a b)").rearrange("p (k t) -> p k t", k=KD)
        kdup = ring[:, 13312:15360].rearrange("p (g t) -> p g t", g=2)

        km = sb("km", [P, 2, MEM])
        vm = sb("vm", [P, 2, MEM])
        sqtmp = sb("sqtmp", [P, 2, S])
        band = sb("band", [P, 2, 2 * P])
        ident = sb("ident", [P, P])
        ones = sb("ones", [P, P])
        headones = sb("headones", [P, P])
        gate_w = sb("gate_w", [P, 2, LT, P])
        w_rt = sb("w_rt", [P, KD, E])
        b_rt = sb("b_rt", [P, E])
        sinkb = sb("sinkb", [P, NQ])
        vecs = sb("vecs", [P, 64])
        st = sb("st", [P, 128])
        vrow = sb("vrow", [NCOL, P])

        def col(i, n=1):
            return vecs[:, i:i + n]
        lamt = sb("lamt", [P, 6, LT])

        uflat = uT[:, :, :].rearrange("p a b -> p (a b)")
        xrow = [uT[:, GATE + i, :] for i in range(2)]
        gbc = uT[:, GATE + 2, :]
        xrT = [uT[:, 9 + i, :].rearrange("p (k t) -> p k t", k=KD) for i in range(2)]

        lg, ex, mask, tmpe = (sqtmp[:, 1, i * NT * E:(i + 1) * NT * E].rearrange("p (t e) -> p t e", t=NT)
                              for i in range(4))
        gates, posm = (a[:, :, :].rearrange("p a b -> p (a b)")[:, 0:NT * E].rearrange("p (t e) -> p t e", t=NT)
                       for a in (km, vm))
        maskb = sb("maskb", [P, NT, E], BF16)
        top8 = sb("top8", [P, NT, 8])
        idx8 = sb("idx8", [P, NT, 8], U32)
        idxf = sb("idxf", [P, NT, 8])
        iota_e = sb("iota_e", [P, E])
        iota_p = sb("iota_p", [P, 1])
        tri = sb("tri", [P, P], BF16)
        onesb = sb("onesb", [P, P], BF16)
        tokid = sb("tokid", [P, NT], F16)
        gatesT, b2_sb = uT[0:E, 6, :], uT[0:E, 7, :]
        cnt = sb("cnt", [P, E])
        nchunk = sb("nchunk", [P, E])
        cum = sb("cum", [P, E])
        ctab = sb("ctab", [P, 2])
        ttab = sb("ttab", [1, 2 * P + E], I32)

        def over(tile, base, n):
            return tile[:, base:base + n]
        xflat = xh[:, :, :].rearrange("p a b -> p (a b)")
        xg = over(uflat, 0, XW)
        xgT = over(uflat, 1088, 1024).rearrange("p (k t) -> p k t", k=KD)
        actT = over(uflat, 2112, 1024).rearrange("p (k t) -> p k t", k=KD)
        rows = over(uflat, 3136, 1024)
        hb = over(uflat, 4160, 1024).rearrange("p (b c) -> p b c", b=2)
        glu = over(uflat, 5184, 512).rearrange("p (b c) -> p b c", b=2)
        lin = over(uflat, 5696, 512).rearrange("p (b c) -> p b c", b=2)
        sig = over(uflat, 6208, 512).rearrange("p (b c) -> p b c", b=2)
        act = over(uflat, 6720, 512).rearrange("p (b c) -> p b c", b=2)
        onehot = over(uflat, 7232, 512).bitcast(F16).rearrange("p (i s) -> p i s", i=NT)
        iota_s = over(uflat, 7744, S + P)
        b1b = over(xflat, 0, 4 * FF)
        grp = sb("grp", [P, 24])
        credit = sb("credit", [P, 4])
        idx_next = sb("idx_next", [P, 1], I32)
        idx_cur = sb("idx_cur", [P, 1], I32)
        pad = sb("pad", [P, 1])
        gate_cur = sb("gate_cur", [P, 1])

        ps = ctx.enter_context(nc.psum_tensor("ps", [P, 8, HALF], F32))

        mem_in, w_mem_in, vec_in, rt_in, wout_in, kdup_in, b2_in, gbc_in = map(
            sem, "mem_in w_mem_in vec_in rt_in wout_in kdup_in b2_in gbc_in".split())
        x_in = [sem(f"x_in{i}") for i in range(2)]
        wA_in = [sem(f"wA_in{i}") for i in range(2)]
        wB_in = [sem(f"wB_in{i}") for i in range(3)]
        xrow_out = [sem(f"xrow_out{i}") for i in range(2)]
        gates_out, init_out = sem("gates_out"), sem("init_out")
        pool_const = sem("pool_const")
        dve_const = sem("dve_const")
        pool_step, dve_step, act_step = sem("pool_step"), sem("dve_step"), sem("act_step")
        sq_sum = sem("sq_sum")
        ms_ready = sem("ms_ready")
        rt_ready = sem("rt_ready")
        scaled = sem("scaled")
        tr_done, tr_out = sem("tr_done"), sem("tr_out")
        mkv_done, mkv_out = sem("mkv_done"), sem("mkv_out")
        in_done, in_out = sem("in_done"), sem("in_out")
        conv_done = sem("conv_done")
        gate_mm, gate_act = sem("gate_mm"), sem("gate_act")
        ab_ready, frac_ready, root_ready = sem("ab_ready"), sem("frac_ready"), sem("root_ready")
        gelu_done, ylru, lru_sq, lru_ss = sem("gelu_done"), sem("ylru"), sem("lru_sq"), sem("lru_ss")
        nsq, nss, nroot, normed = sem("nsq"), sem("nss"), sem("nroot"), sem("normed")
        sc_done, sc_out, nmx_ready, exp_done, sink_in, sink_exp = map(
            sem, "sc_done sc_out nmx_ready exp_done sink_in sink_exp".split())
        pt_done, pt_act, pt_dve, pv_done, o_ready, o_ss, yt_done, yt_out = map(
            sem, "pt_done pt_act pt_dve pv_done o_ready o_ss yt_done yt_out".split())
        grp_ms, grp_root, grp_rs = sem("grp_ms"), sem("grp_root"), sem("grp_rs")
        op_done, op_out, h_sq, h_ms, h_root, xr_ready = map(
            sem, "op_done op_out h_sq h_ms h_root xr_ready".split())
        xt_done, xt_out, lg_done, lg_out = map(sem, "xt_done xt_out lg_done lg_out".split())
        ex_in, ex_done, mask_ready, pos_done, gates_ready, gt_done, gt_out, init_mm, init_ready = map(
            sem, "ex_in ex_done mask_ready pos_done gates_ready gt_done gt_out init_mm init_ready".split())
        ctab_ready, ttab_ps, ttab_ready = sem("ctab_ready"), sem("ttab_ps"), sem("ttab_ready")
        slot_in = [sem(f"slot_in{i}") for i in range(NSLOT)]
        w_used, b1_in = sem("w_used"), sem("b1_in")
        onehot_ready, ids_done, idx_ready, idxcur_ready, gate_copied = map(
            sem, "onehot_ready ids_done idx_ready idxcur_ready gate_copied".split())
        xg_in, xgt_done, xgT_ready, rows_in, scattered = map(
            sem, "xg_in xgt_done xgT_ready rows_in scattered".split())
        h_free, glu_ready, lin_ready, sig_ready, act_ready, at_done, actT_ready, combined = map(
            sem, "h_free glu_ready lin_ready sig_ready act_ready at_done actT_ready combined".split())
        vec_ps, vec_ready, lam_in, lam_exp, gw_in, lin_done = map(
            sem, "vec_ps vec_ready lam_in lam_exp gw_in lin_done".split())
        zeroed, moe_step = sem("zeroed"), sem("moe_step")

        units = [(h, c) for h in range(2) for c in range(6)]
        units += [(h, c) for c in (K, V) for h in range(2)] + [(h, c) for c in (Q, Q + 1, Q + 2, QM, QM + 1) for h in range(2)]
        upos = {u: i for i, u in enumerate(units)}
        normt = [(uT[:, K, :], S, C_KS), (km[:, :, :].rearrange("p a b -> p (a b)"), 2 * MEM, C_KM)]
        normt += [(uT[:, Q + i, :], S, C_QS) for i in range(3)] + [(uT[:, QM + i, :], S, C_QM) for i in range(2)]
        nssc = [0]
        for _, w, _ in normt:
            nssc.append(nssc[-1] + w // HALF)
        items = [(kind, b) for b in range(NT) for kind in ("swa", "mem")]

        def heads(kind):
            return NQ if kind == "swa" else NM

        def score_banks(kind):
            return [(0, 2), (1, 3), (4,), (5,)] if kind == "swa" else [(0, 2), (1, 3)]

        scb, hc, ytc = [0], [0], [0]
        for kind, _ in items:
            scb.append(scb[-1] + len(score_banks(kind)))
            hc.append(hc[-1] + heads(kind))
            ytc.append(ytc[-1] + heads(kind) // 2)
        ptac = [0]
        for kind, _ in items:
            ptac.append(ptac[-1] + (heads(kind) // 2 + 1) // 2)

        def slot(s):
            return ring[:, s * SLOT:(s + 1) * SLOT].rearrange("p (k c) -> p k c", k=4)

        rank = {0: 1, 1: 2, 2: 3, 3: 4, 4: 5, 5: 6, 6: 7, 7: 8, 8: 9, 10: 10, 9: 11, 11: 12}

        block = ctx.enter_context(nc.Block())

        @block.sync
        def _(sp):
            sp.dma_start(mem_sb, mem[0].rearrange("(t p) d -> p t d", p=P)).then_inc(mem_in, 16)
            xv = x[0].rearrange("(t p) d -> p t d", p=P)
            sp.dma_start(xh[:, 0:4, :], xv[:, 0:4, :]).then_inc(x_in[0], 16)
            sp.dma_start(w_mem, w_mem_kv[0].rearrange("(k p) c -> p k c", p=P)).then_inc(w_mem_in, 16)
            sp.dma_start(xh[:, 4:8, :], xv[:, 4:8, :]).then_inc(x_in[1], 16)
            wv = w_in[0].rearrange("(k p) c -> p k c", p=P)
            for i in range(2):
                sp.dma_start(wA[:, :, i * DL:(i + 1) * DL], wv[:, :, i * DL:(i + 1) * DL]).then_inc(wA_in[i], 16)
            for i, (a, b) in enumerate(((384, 640), (0, 384), (640, 896))):
                sp.dma_start(wB[:, :, a:b], wv[:, :, 768 + a:768 + b]).then_inc(wB_in[i], 16)
            sp.wait_ge(in_done, len(units))
            sp.dma_start(w_out_sb, w_out[0].rearrange("(k p) c -> p k c", p=P)).then_inc(wout_in, 16)
            sp.wait_ge(normed, 1)
            for g in range(2):
                for half in range(2):
                    sp.dma_start(kdup[half * DH:(half + 1) * DH, g, :],
                                 uT[g * DH:(g + 1) * DH, K, :]).then_inc(kdup_in, 16)

            w1v = w1[0].rearrange("e (k p) c -> e p k c", p=P)
            w2v = w2[0].rearrange("e (k p) c -> e p k c", p=P)

            def load_slot(e, s):
                if s < 8:
                    src = w1v[e, :, 4 * (s % 2):4 * (s % 2) + 4, HALF * (s // 2):HALF * (s // 2) + HALF]
                else:
                    src = w2v[e, :, 4 * (s % 2):4 * (s % 2) + 4, HALF * ((s - 8) // 2):HALF * ((s - 8) // 2) + HALF]
                sp.dma_start(slot(s), src).then_inc(slot_in[s], 16)

            sp.wait_ge(ylru, 2 * LT)
            sp.dma_start(gbc, g_ffn.to_broadcast([P, D])).then_inc(gbc_in, 16)
            sp.wait_ge(lru_ss, 1)
            sp.wait_ge(yt_out, ytc[-1])
            sp.wait_ge(o_ss, len(items))
            for s in range(8):
                load_slot(0, s)
            sp.wait_ge(op_done, 6 * NT)
            sp.dma_start(b2_sb, b2[0]).then_inc(b2_in, 16)
            for s in range(8, NSLOT):
                load_slot(0, s)
            for i in range(NT):
                sp.wait_ge(init_ready, 2 * i + 2)
                sp.dma_start(out[0, i * P:(i + 1) * P, :], xh[:, i, :]).then_inc(init_out, 16)
            sp.wait_ge(init_out, 16 * NT)
            sp.wait_ge(ttab_ready, 1)
            sp.dma_start(b1b[:, 0:2 * FF], b1[0, 0:1, :].to_broadcast([P, 2 * FF])).then_inc(b1_in, 16)
            sp.wait_ge(b1_in, 16)
            sp.dma_start(b1b[:, 2 * FF:4 * FF], b1[0, 1:2, :].to_broadcast([P, 2 * FF])).then_inc(b1_in, 16)
            used_reg, e16_reg, hf_reg = (sp.alloc_register(n) for n in ("used", "e16", "hf"))
            with sp.Fori(1, E) as e:
                before = sp.value_load(ttab[0:1, bass.ds(2 * P + e - 1, 1)], min_val=0, max_val=NCH)
                sp.reg_mul(used_reg, before, NSLOT)
                sp.reg_mul(e16_reg, e, 16)
                e16 = sp.snap(e16_reg)
                for s in sorted(range(NSLOT), key=lambda s: rank[s]):
                    sp.reg_add(used_reg, used_reg, 1)
                    used = sp.snap(used_reg)
                    sp.wait_ge(slot_in[s], e16)
                    sp.wait_ge(w_used, used)
                    if s < 8:
                        src = w1v[bass.ds(e, 1), :, 4 * (s % 2):4 * (s % 2) + 4, HALF * (s // 2):HALF * (s // 2) + HALF]
                    else:
                        src = w2v[bass.ds(e, 1), :, 4 * (s % 2):4 * (s % 2) + 4, HALF * ((s - 8) // 2):HALF * ((s - 8) // 2) + HALF]
                    sp.dma_start(slot(s), src.rearrange("o p k c -> (o p) k c")).then_inc(slot_in[s], 16)
                nxt = sp.snap((e + 1) % E, min_val=0, max_val=E - 1)
                dst = sp.snap((e + 1) % 2 * (2 * FF), min_val=0, max_val=2 * FF)
                sp.reg_mul(hf_reg, before, 4)
                sp.reg_add(hf_reg, hf_reg, 4)
                hf = sp.snap(hf_reg)
                sp.reg_add(e16_reg, e16_reg, 16)
                e16 = sp.snap(e16_reg)
                sp.wait_ge(h_free, hf)
                sp.wait_ge(b1_in, e16)
                sp.dma_start(b1b[:, bass.ds(dst, 2 * FF)],
                             b1[0, bass.ds(nxt, 1), :].to_broadcast([P, 2 * FF])).then_inc(b1_in, 16)
            sp.wait_ge(b1_in, 16 * (E + 1))
            for s in range(NSLOT):
                sp.wait_ge(slot_in[s], 16 * E)

        @block.gpsimd
        def _(po):
            po.memset(ident[:, :], 0.0).then_inc(pool_step, 1)
            po.memset(ones[:, :], 1.0).then_inc(pool_step, 1)
            po.memset(headones[:, :], 0.0).then_inc(pool_step, 1)
            po.memset(band[:, :, :], 0.0).then_inc(pool_step, 1)
            po.memset(onesb[:, :], 1.0).then_inc(pool_step, 1)
            po.memset(gate_w[:, :, :, :], 0.0).then_inc(pool_step, 1)
            po.wait_ge(pool_step, 6)
            po.affine_select(out=ident[:, :], in_=ident[:, :], compare_op=ALU.not_equal, fill=1.0, base=0,
                             pattern=[[-1, P]], channel_multiplier=1).then_inc(pool_const, 1)
            for half in range(2):
                po.wait_ge(pool_const, half + 1)
                po.memset(headones[half * DH:(half + 1) * DH, half * DH:(half + 1) * DH], 1.0).then_inc(pool_const, 1)
            po.wait_ge(pool_const, 3)
            po.affine_select(out=band[:, :, P:2 * P], in_=band[:, :, P:2 * P], compare_op=ALU.is_ge, fill=-1e30,
                             base=0, pattern=[[0, 2], [-1, P]], channel_multiplier=1).then_inc(pool_const, 1)
            po.affine_select(out=band[:, 0, 0:P], in_=band[:, 0, 0:P], compare_op=ALU.is_gt, fill=-1e30,
                             base=0, pattern=[[1, P]], channel_multiplier=-1).then_inc(pool_const, 1)
            po.memset(band[:, 1, 0:P], -1e30).then_inc(pool_const, 1)
            po.affine_select(out=tri[:, :], in_=onesb[:, :], compare_op=ALU.is_gt, fill=0.0, base=0,
                             pattern=[[1, P]], channel_multiplier=-1).then_inc(pool_const, 1)
            po.iota(iota_e[:, :], [[1, E]], base=0, channel_multiplier=0,
                    allow_small_or_imprecise_dtypes=True).then_inc(pool_const, 1)
            po.iota(iota_p[:, :], [[0, 1]], base=0, channel_multiplier=1,
                    allow_small_or_imprecise_dtypes=True).then_inc(pool_const, 1)
            po.iota(tokid[:, :], [[P, NT]], base=1, channel_multiplier=1,
                    allow_small_or_imprecise_dtypes=True).then_inc(pool_const, 1)
            for g, w in enumerate((lru_wa, lru_wx)):
                for half in range(2):
                    po.dma_start(gate_w[half * DH:(half + 1) * DH, g, :, half * DH:(half + 1) * DH],
                                 w[0, half::2].rearrange("h i j -> i h j")).then_inc(gw_in, 16)
            po.dma_start(b_rt[:, :], b_router.to_broadcast([P, E])).then_inc(rt_in, 16)
            po.dma_start(sinkb[:, :], swa_sinks.to_broadcast([P, NQ])).then_inc(rt_in, 16)
            po.dma_start(w_rt[:, :, :], w_router[0].rearrange("(k p) c -> p k c", p=P)).then_inc(rt_in, 16)

            for i in range(NT):
                po.wait_ge(xr_ready, i + 1)
                po.dma_start(xrows[i * P:(i + 1) * P, 0:D], xrow[i % 2]).then_inc(xrow_out[i % 2], 16)
            po.wait_ge(gates_ready, 1)
            po.dma_start(xrows.rearrange("(t p) c -> p t c", p=P)[:, :, D:XW], gates[:, :, :]).then_inc(gates_out, 16)

            po.wait_ge(init_ready, 2 * NT)
            for i in range(2):
                po.wait_ge(xrow_out[i], 16 * NT // 2)
            po.wait_ge(gates_out, 16)
            po.memset(xg, 0.0).then_inc(zeroed, 1)
            po.memset(rows, 0.0).then_inc(zeroed, 1)
            po.iota(iota_s, [[1, S + P]], base=0, channel_multiplier=0,
                    allow_small_or_imprecise_dtypes=True).then_inc(zeroed, 1)

            none_reg, last_row = po.alloc_register("none"), po.alloc_register("last_row")
            po.reg_mov(none_reg, 0)

            def gather_x():
                po.wait_ge(zeroed, 3)
                po.reg_add(last_row, none_reg, S - 1)
                po.indirect_dma_start(out=xg, out_offset=None, in_=xrows[:, :],
                                      in_offset=bass.IndirectOffsetOnAxis(ap=idx_next[:, 0:1], axis=0),
                                      bounds_check=last_row, oob_is_err=False).then_inc(xg_in, 16)

            po.wait_ge(idx_ready, 1)
            gather_x()
            po.wait_ge(ttab_ready, 1)
            total = po.value_load(ttab[0:1, 2 * P + E - 1:2 * P + E], min_val=1, max_val=NCH)
            with po.Fori(0, total) as c:
                po.tensor_copy(idx_cur[:, :], idx_next[:, :]).then_inc(idxcur_ready, 1)
                po.wait_ge(idxcur_ready, c + 1)
                po.wait_ge(init_out, 16 * NT)
                po.reg_add(last_row, none_reg, S - 1)
                po.indirect_dma_start(out=rows, out_offset=None, in_=out[0],
                                      in_offset=bass.IndirectOffsetOnAxis(ap=idx_cur[:, 0:1], axis=0),
                                      bounds_check=last_row, oob_is_err=False).then_inc(rows_in, 16)
                po.wait_ge(idx_ready, c + 2)
                po.wait_ge(xgt_done, c * 2 + 2)
                po.wait_ge(gate_copied, c + 1)
                gather_x()
                po.wait_ge(combined, c * 2 + 4)
                po.reg_add(last_row, none_reg, S - 1)
                po.indirect_dma_start(out=out[0], out_offset=bass.IndirectOffsetOnAxis(ap=idx_cur[:, 0:1], axis=0),
                                      in_=rows, in_offset=None,
                                      bounds_check=last_row, oob_is_err=False).then_inc(scattered, 16)
                po.wait_ge(scattered, c * 16 + 16)
            po.wait_ge(xg_in, total * 16 + 16)

        @block.scalar
        def _(act_e):
            for base, v, k in ((C_GMIX, g_mix, KD), (C_GMEM, g_mem, KD), (C_CONVB, conv_b, LT), (C_BA, lru_ba, LT),
                               (C_BX, lru_bx, LT), (C_LAM, lru_lambda, LT), (C_GOL, g_out_lru, LT),
                               (C_GOS, g_out_swa, LT), (C_GOM, g_out_mem, 2)):
                act_e.dma_start(vrow[base:base + k, :], v[0].rearrange("(k p) -> k p", p=P)).then_inc(vec_in, 16)
            act_e.dma_start(vrow[C_CONVW:C_CONVW + 12, :], conv_w[0].rearrange("w (k p) -> (w k) p", p=P)).then_inc(vec_in, 16)
            for base, v in ((C_QS, q_norm_swa), (C_KS, k_norm_swa), (C_QM, q_norm_mem), (C_KM, k_norm_mem)):
                for half in range(2):
                    act_e.dma_start(vrow[base:base + 1, half * DH:(half + 1) * DH], v).then_inc(vec_in, 16)
            act_e.wait_ge(mem_in, 16)
            for t in range(2):
                if t:
                    act_e.wait_ge(sq_sum, 1)
                act_e.activation(sqscr, mem_sb[:, t, :], ACT.Square, accum_out=st[:, t:t + 1]).then_inc(sq_sum, 1)
            act_e.wait_ge(lam_in, 1)
            act_e.activation(lamt[:, 1, :], lamt[:, 1, :], ACT.Exp).then_inc(lam_exp, 1)
            for h in range(2):
                act_e.wait_ge(x_in[h], 16)
                for t in range(4):
                    i = 4 * h + t
                    act_e.wait_ge(sq_sum, i + 2)
                    act_e.activation(sqscr, xh[:, i, :], ACT.Square,
                                     accum_out=st[:, 2 + i:3 + i]).then_inc(sq_sum, 1)
            for n, (a, b) in enumerate(((0, 2), (2, 6), (6, 10))):
                act_e.wait_ge(ms_ready, n + 1)
                act_e.activation(st[:, 32 + a:32 + b], st[:, 16 + a:16 + b], ACT.Sqrt).then_inc(rt_ready, 1)
            for u in range(4):
                act_e.wait_ge(mkv_done, u + 1)
                dst = km[:, u, :] if u < 2 else vm[:, u - 2, :]
                act_e.activation(dst, ps[:, u, 0:MEM], ACT.Copy).then_inc(mkv_out, 1)

            def take_unit(i):
                h, c = units[i]
                act_e.wait_ge(in_done, i + 1)
                if i == 0:
                    act_e.wait_ge(sq_sum, 10)
                act_e.activation(uT[:, c, h * HALF:(h + 1) * HALF], ps[:, i % 4, :], ACT.Copy).then_inc(in_out, 1)

            def lru_gates(c):
                for g, bias in ((0, C_BA), (1, C_BX)):
                    for h in range(2):
                        act_e.wait_ge(gate_mm, 4 * c + 2 * g + h + 1)
                        if c and g == 0 and h == 0:
                            act_e.wait_ge(ylru, 2 * c)
                        act_e.activation(lru_tmp[:, 1 + g, h * HALF:(h + 1) * HALF], ps[:, 4 + 2 * g + h, :], ACT.Sigmoid,
                                         bias=col(bias + c)).then_inc(gate_act, 1)
                act_e.wait_ge(gate_act, 4 * c + 2)
                act_e.activation(lru_tmp[:, 3, :], lru_tmp[:, 1, :], ACT.Tanh, scale=col(C_SP8 + c)).then_inc(ab_ready, 1)
                act_e.activation(lru_tmp[:, 4, :], lru_tmp[:, 1, :], ACT.Exp, scale=col(C_NSP8 + c)).then_inc(ab_ready, 1)
                act_e.wait_ge(frac_ready, c + 1)
                act_e.activation(lru_tmp[:, 3, :], lru_tmp[:, 3, :], ACT.Sqrt).then_inc(root_ready, 1)
                act_e.wait_ge(in_out, upos[(1, GATE + c)] + 1)
                act_e.activation(uT[:, GATE + c, :], uT[:, GATE + c, :], ACT.Gelu_apprx_tanh).then_inc(gelu_done, 1)

            nA = 12
            for i in range(nA):
                take_unit(i)
            act_e.wait_ge(dve_const, 1)
            left = list(range(nA, len(units)))
            for c in range(LT):
                for i in left[5 * c:5 * c + 5]:
                    take_unit(i)
                lru_gates(c)
            assert not left[15:]

            for n, (t, w, g) in enumerate(normt):
                if n == 0:
                    act_e.wait_ge(mkv_out, 4)
                    act_e.wait_ge(in_out, len(units))
                if n >= 2:
                    act_e.wait_ge(normed, n - 1)
                act_e.activation(sqtmp[:, n % 2, 0:w], t, ACT.Square).then_inc(nsq, 1)
                for h in range(w // HALF):
                    act_e.wait_ge(nss, nssc[n] + h + 1)
                    act_e.activation(sqtmp[:, n % 2, h * HALF:(h + 1) * HALF], ps[:, 4 + (nssc[n] + h) % 4, :],
                                     ACT.Sqrt, bias=col(C_EPS), scale=1.0 / DH).then_inc(nroot, 1)

            def exps(j):
                kind, b = items[j]
                nh = heads(kind)
                act_e.wait_ge(nmx_ready, j + 1)
                for h in range(nh):
                    act_e.activation(scores_sb[:, j % 2, h, :], scores_sb[:, j % 2, h, :], ACT.Exp,
                                     bias=st[:, 48 + 8 * (j % 2) + h:49 + 8 * (j % 2) + h],
                                     accum_out=st[:, 64 + 8 * (j % 2) + h:65 + 8 * (j % 2) + h]).then_inc(exp_done, 1)
                if kind == "swa":
                    act_e.wait_ge(sink_in, b + 1)
                    act_e.activation(st[:, 80:86], st[:, 80:86], ACT.Exp).then_inc(sink_exp, 1)

            def take_probs(j):
                kind, b = items[j]
                for k in range(0, heads(kind) // 2, 2):
                    act_e.wait_ge(pt_done, ytc[j] + k + 1)
                    if j:
                        act_e.wait_ge(pv_done, j)
                    act_e.activation(probsT[:, 4 * k:4 * k + 4, :], ps[:, 4, :].rearrange("p (a b) -> p a b", a=4),
                                     ACT.Copy).then_inc(pt_act, 1)

            def take_o(j):
                kind, b = items[j]
                w = heads(kind) * DH
                act_e.wait_ge(o_ready, j + 1)
                if j:
                    act_e.wait_ge(o_ss, j)
                act_e.activation(o_sq[:, 0:w], o_sb[:, j % 2, 0:w], ACT.Square,
                                 accum_out=st[:, 96 + j:97 + j]).then_inc(o_ss, 1)

            for j in range(len(items) + 1):
                if j < len(items):
                    exps(j)
                if j >= 1:
                    take_probs(j - 1)
                    take_o(j - 1)
            act_e.wait_ge(grp_ms, 1)
            act_e.activation(grp[:, 0:24], grp[:, 0:24], ACT.Sqrt).then_inc(grp_root, 1)
            for i in range(NT):
                act_e.wait_ge(op_out, 6 * i + 6)
                if i:
                    act_e.wait_ge(h_sq, i)
                act_e.activation(sqtmp[:, 0, :], xh[:, i, :], ACT.Square, accum_out=st[:, i:i + 1]).then_inc(h_sq, 1)
                act_e.wait_ge(h_ms, i + 1)
                act_e.activation(st[:, 16 + i:17 + i], st[:, 8 + i:9 + i], ACT.Sqrt).then_inc(h_root, 1)
                for m in range(2):
                    act_e.wait_ge(xt_done, 2 * i + m + 1)
                    if i >= 2:
                        act_e.wait_ge(lg_done, i - 1)
                    act_e.activation(xrT[i % 2][:, 4 * m:4 * m + 4, :],
                                     ps[:, 6, :].rearrange("p (a b) -> p a b", a=4), ACT.Copy).then_inc(xt_out, 1)
            act_e.wait_ge(ex_in, 1)
            act_e.activation(ex[:, :, :], ex[:, :, :], ACT.Exp).then_inc(ex_done, 1)
            for i in range(2):
                act_e.wait_ge(gt_done, 4 * i + 4)
                act_e.activation(gatesT[:, i * HALF:(i + 1) * HALF], ps[0:E, i, :], ACT.Copy).then_inc(gt_out, 1)

            def take_xgT(base):
                for m in range(2):
                    act_e.wait_ge(xgt_done, base + m + 1)
                    act_e.activation(xgT[:, 4 * m:4 * m + 4, :], ps[:, 6 + m, :].rearrange("p (a b) -> p a b", a=4),
                                     ACT.Copy).then_inc(xgT_ready, 1)

            act_e.wait_ge(ttab_ready, 1)
            total = act_e.value_load(ttab[0:1, 2 * P + E - 1:2 * P + E], min_val=1, max_val=NCH)
            take_xgT(0)
            with act_e.Fori(0, total) as c:
                c4 = act_e.snap(c * 4)
                c2 = act_e.snap(c * 2 + 2)

                def sigmoid(j):
                    act_e.wait_ge(glu_ready, c4 + (j + 1))
                    if j >= 2:
                        act_e.wait_ge(act_ready, c4 + (j - 1))
                    act_e.activation(sig[:, j % 2, :], glu[:, j % 2, :], ACT.Sigmoid, scale=ALPHA).then_inc(sig_ready, 1)

                def take_actT(j):
                    act_e.wait_ge(at_done, c4 + (j + 1))
                    act_e.activation(actT[:, 2 * j:2 * j + 2, :], ps[:, 7, 0:2 * P].rearrange("p (a b) -> p a b", a=2),
                                     ACT.Copy).then_inc(actT_ready, 1)

                sigmoid(0)
                sigmoid(1)
                take_actT(0)
                sigmoid(2)
                take_actT(1)
                sigmoid(3)
                take_actT(2)
                take_actT(3)
                take_xgT(c2)

        @block.tensor
        def _(pe):
            pe.wait_ge(pool_const, 1)
            pe.wait_ge(vec_in, 16 * NVEC)
            pe.transpose(ps[:, 0, 0:NCOL], vrow[:, :], ident[0:NCOL, 0:NCOL]).then_inc(vec_ps, 1)
            tb = [0]

            def bank_of_transposes():
                n = tb[0]
                tb[0] += 1
                if n >= 4:
                    pe.wait_ge(tr_out, n - 3)
                return 4 + n % 4

            pe.wait_ge(scaled, 1)
            for k in range(0, KD, 2):
                b = bank_of_transposes()
                for kk in range(2):
                    for t in range(2):
                        m = pe.transpose(ps[:, b, kk * MEM + t * P:kk * MEM + (t + 1) * P],
                                         ms[:, t, (k + kk) * P:(k + kk + 1) * P], ident[:, :])
                m.then_inc(tr_done, 1)

            def x_transposes(h):
                pe.wait_ge(scaled, 2 + h)
                for k in range(KD):
                    b = bank_of_transposes()
                    for t in range(4):
                        m = pe.transpose(ps[:, b, t * P:(t + 1) * P], xs[:, t, k * P:(k + 1) * P], ident[:, :])
                    m.then_inc(tr_done, 1)

            x_transposes(0)
            pe.wait_ge(w_mem_in, 16)
            pe.wait_ge(tr_out, 4)
            pe.wait_ge(vec_ready, 1)
            for u in range(4):
                for k in range(KD):
                    if u < 2:
                        m = pe.matmul(ps[:, u, 0:MEM], w_mem[:, k, u * P:(u + 1) * P], memT_v[:, k, :],
                                      start=k == 0, stop=k == KD - 1)
                    else:
                        m = pe.matmul(ps[:, u, 0:MEM], memT_v[:, k, (u - 2) * P:(u - 1) * P], w_mem[:, k, MEM:2 * MEM],
                                      start=k == 0, stop=k == KD - 1)
                m.then_inc(mkv_done, 1)
            x_transposes(1)

            def unit(i):
                h, c = units[i]
                if i < 4:
                    pe.wait_ge(mkv_out, i + 1)
                else:
                    pe.wait_ge(in_out, i - 3)
                pe.wait_ge(tr_out, 4 + 8 * (h + 1))
                if c < 6:
                    pe.wait_ge(wA_in[c // 3], 16)
                    w = wA[:, :, c * P:(c + 1) * P]
                else:
                    pe.wait_ge(wB_in[{K: 0, V: 0, Q: 1, Q + 1: 1, Q + 2: 1}.get(c, 2)], 16)
                    w = wB[:, :, (c - 6) * P:(c - 5) * P]
                if c == V:
                    for t in range(4):
                        for k in range(KD):
                            m = pe.matmul(ps[:, i % 4, t * P:(t + 1) * P], xnT[:, k, (4 * h + t) * P:(4 * h + t + 1) * P],
                                          w[:, k, :], start=k == 0, stop=k == KD - 1)
                else:
                    for k in range(KD):
                        m = pe.matmul(ps[:, i % 4, :], w[:, k, :], xnT[:, k, h * HALF:(h + 1) * HALF],
                                      start=k == 0, stop=k == KD - 1)
                m.then_inc(in_done, 1)

            def gate_products(c):
                pe.wait_ge(conv_done, c + 1)
                pe.wait_ge(gw_in, 64)
                if c == 0:
                    pe.wait_ge(tr_out, 20)
                else:
                    pe.wait_ge(gate_act, 4 * c)
                for g in range(2):
                    for h in range(2):
                        pe.matmul(ps[:, 4 + 2 * g + h, :], gate_w[:, g, c, :], lru_tmp[:, 0, h * HALF:(h + 1) * HALF],
                                  start=True, stop=True).then_inc(gate_mm, 1)

            for i in range(12):
                unit(i)
            for c in range(LT):
                for i in range(12 + 5 * c, min(12 + 5 * c + 5, len(units))):
                    unit(i)
                gate_products(c)
            pe.wait_ge(pool_const, NPOOLC)
            pe.wait_ge(gate_act, 4 * LT)
            for n, (t, w, g) in enumerate(normt):
                pe.wait_ge(nsq, n + 1)
                for h in range(w // HALF):
                    u = nssc[n] + h
                    if u >= 4:
                        pe.wait_ge(nroot, u - 3)
                    pe.matmul(ps[:, 4 + u % 4, :], headones[:, :], sqtmp[:, n % 2, h * HALF:(h + 1) * HALF],
                              start=True, stop=True).then_inc(nss, 1)
            pe.wait_ge(normed, len(normt))
            pe.wait_ge(nroot, nssc[-1])
            pe.wait_ge(kdup_in, 64)

            def scores(j):
                kind, b = items[j]
                for k, hs in enumerate(score_banks(kind)):
                    if j:
                        pe.wait_ge(sc_out, min(scb[j - 1] + k + 1, scb[j]))
                    for n, h in enumerate(hs):
                        o = (h % 2) * DH
                        lo = P if kind == "swa" and b == 0 else 0
                        if kind == "swa":
                            qs = uT[o:o + DH, Q + h // 2, b * P:(b + 1) * P]
                            keys = kdup[o:o + DH, h // 3, (b - 1) * P + lo:(b + 1) * P]
                        else:
                            qs = uT[o:o + DH, QM + h // 2, b * P:(b + 1) * P]
                            keys = km[o:o + DH, h // 2, :]
                        m = pe.matmul(ps[:, k, n * 256 + lo:n * 256 + 256], qs, keys, start=True, stop=True)
                    m.then_inc(sc_done, 1)

            def transpose_probs(j):
                kind, b = items[j]
                for k in range(heads(kind) // 2):
                    pe.wait_ge(exp_done, hc[j] + 2 * k + 2)
                    if k % 2 == 0:
                        if ptac[j] + k // 2:
                            pe.wait_ge(pt_act, ptac[j] + k // 2)
                    elif j:
                        pe.wait_ge(pt_dve, j)
                    for a in range(4):
                        h, part = 2 * k + a // 2, a % 2
                        m = pe.transpose(ps[:, 4 + k % 2, a * P:(a + 1) * P], scores_sb[:, j % 2, h, part * P:(part + 1) * P],
                                         ident[:, :])
                    m.then_inc(pt_done, 1)

            def values(j):
                kind, b = items[j]
                pe.wait_ge(pt_act, ptac[j + 1])
                pe.wait_ge(pt_dve, j + 1)
                if j:
                    pe.wait_ge(o_ready, j)
                for h in range(heads(kind)):
                    parts = [1] if kind == "swa" and b == 0 else [0, 1]
                    for part in parts:
                        if kind == "swa":
                            v = uT[:, V, (b - 1 + part) * P + (h // 3) * DH:(b - 1 + part) * P + (h // 3 + 1) * DH]
                        else:
                            v = vm[:, part, h * DH:(h + 1) * DH]
                        m = pe.matmul(ps[:, 6, h * DH:(h + 1) * DH], probsT[:, 2 * h + part, :], v,
                                      start=part == parts[0], stop=part == 1)
                m.then_inc(pv_done, 1)

            def transpose_o(j):
                kind, b = items[j]
                pe.wait_ge(o_ready, j + 1)
                if j:
                    pe.wait_ge(yt_out, ytc[j])
                for t in range(heads(kind) // 2):
                    m = pe.transpose(ps[:, 7, t * P:(t + 1) * P], o_sb[:, j % 2, t * P:(t + 1) * P], ident[:, :])
                m.then_inc(yt_done, 1)

            for j in range(len(items) + 1):
                if j < len(items):
                    scores(j)
                if j >= 1:
                    transpose_probs(j - 1)
                    values(j - 1)
                    transpose_o(j - 1)
            pe.wait_ge(lru_sq, LT)
            for i in range(NT):
                for c in range(LT):
                    m = pe.matmul(ps[:, 0, i:i + 1], lru_tmp[:, 3 + c, i * P:(i + 1) * P], ones[:, 0:1],
                                  start=c == 0, stop=c == LT - 1)
            m.then_inc(lru_ss, 1)

            groups = ([LRU, LRU + 1, LRU + 2], [Q, Q + 1, Q + 2], [QM, QM + 1])
            pe.wait_ge(wout_in, 16)
            pe.wait_ge(grp_ms, 1)
            pe.wait_ge(yt_out, ytc[-1])
            pe.wait_ge(rt_in, 16 * NRT)

            def project(i):
                kk = 0
                for g, tiles in enumerate(groups):
                    for half in range(2):
                        if i:
                            pe.wait_ge(op_out, 6 * (i - 1) + 2 * g + half + 1)
                        for n, c in enumerate(tiles):
                            m = pe.matmul(ps[:, 2 * g + half, :], uT[:, c, i * P:(i + 1) * P],
                                          w_out_sb[:, kk + n, half * HALF:(half + 1) * HALF],
                                          start=n == 0, stop=n == len(tiles) - 1)
                        m.then_inc(op_done, 1)
                    kk += len(tiles)

            def route(i):
                pe.wait_ge(xr_ready, i + 1)
                for m2 in range(2):
                    if 2 * i + m2:
                        pe.wait_ge(xt_out, 2 * i + m2)
                    for a in range(4):
                        m = pe.transpose(ps[:, 6, a * P:(a + 1) * P], xrow[i % 2][:, (4 * m2 + a) * P:(4 * m2 + a + 1) * P],
                                         ident[:, :])
                    m.then_inc(xt_done, 1)
                pe.wait_ge(xt_out, 2 * i + 2)
                if i:
                    pe.wait_ge(lg_out, i)
                for k in range(KD):
                    m = pe.matmul(ps[:, 7, 0:E], xrT[i % 2][:, k, :], w_rt[:, k, :], start=k == 0, stop=k == KD - 1)
                m.then_inc(lg_done, 1)

            for i in range(NT + 1):
                if i < NT:
                    project(i)
                if i >= 1:
                    route(i - 1)

            pe.wait_ge(mask_ready, 1)
            pe.wait_ge(op_out, 6 * NT)
            for i in range(NT):
                for j in range(i + 1):
                    m = pe.matmul(ps[:, 2, i * E:(i + 1) * E], onesb[:, :] if j < i else tri[:, :], maskb[:, j, :],
                                  start=j == 0, stop=j == i)
            for j in range(NT):
                m = pe.matmul(ps[:, 3, 0:E], onesb[:, :], maskb[:, j, :], start=j == 0, stop=j == NT - 1)
            m.then_inc(pos_done, 1)
            pe.wait_ge(ctab_ready, 1)
            for a in range(2):
                m = pe.transpose(ps[0:1, 4, a * P:(a + 1) * P], ctab[:, a:a + 1], ident[:, :])
            m.then_inc(ttab_ps, 1)
            pe.wait_ge(gates_ready, 1)
            for i in range(NT):
                pe.transpose(ps[0:E, i // 4, (i % 4) * P:(i % 4 + 1) * P], gates[:, i, :], ident[:, :]).then_inc(gt_done, 1)
            pe.wait_ge(gt_out, 2)
            pe.wait_ge(b2_in, 16)
            for i in range(NT):
                for half in range(2):
                    u = 2 * i + half
                    if u >= 2:
                        pe.wait_ge(init_ready, u - 1)
                    pe.matmul(ps[:, 5 + u % 2, :], gatesT[:, i * P:(i + 1) * P], b2_sb[:, half * HALF:(half + 1) * HALF],
                              start=True, stop=True).then_inc(init_mm, 1)

            def token_ids(n):
                pe.wait_ge(onehot_ready, n)
                for i in range(NT):
                    m = pe.matmul(ps[:, 6, 0:1], onehot[:, i, :], tokid[:, i:i + 1], start=i == 0, stop=i == NT - 1)
                m.then_inc(ids_done, 1)

            def transpose_x(n16):
                pe.wait_ge(xg_in, n16)
                for m2 in range(2):
                    for a in range(4):
                        m = pe.transpose(ps[:, 6 + m2, a * P:(a + 1) * P], xg[:, (4 * m2 + a) * P:(4 * m2 + a + 1) * P],
                                         ident[:, :])
                    m.then_inc(xgt_done, 1)

            pe.wait_ge(init_ready, 2 * NT)
            pe.wait_ge(ttab_ready, 1)
            total = pe.value_load(ttab[0:1, 2 * P + E - 1:2 * P + E], min_val=1, max_val=NCH)
            token_ids(1)
            pe.wait_ge(idx_ready, 1)
            transpose_x(16)
            with pe.Fori(0, total) as c:
                e = pe.value_load(ttab[0:1, bass.ds(c, 1)], min_val=0, max_val=E - 1)
                e16 = pe.snap(e * 16 + 16)
                c2 = pe.snap(c * 2)
                c4 = pe.snap(c * 4)

                def transpose_act(j):
                    pe.wait_ge(act_ready, c4 + (j + 1))
                    if j:
                        pe.wait_ge(actT_ready, c4 + j)
                    for a in range(2):
                        m = pe.transpose(ps[:, 7, a * P:(a + 1) * P], act[:, j % 2, a * P:(a + 1) * P], ident[:, :])
                    m.then_inc(at_done, 1)

                pe.wait_ge(xgT_ready, c2 + 2)
                for j in range(4):
                    pe.wait_ge(h_free, c4 + (j + 1))
                    for k in range(KD):
                        s = 2 * j + k // 4
                        if k % 4 == 0:
                            pe.wait_ge(slot_in[s], e16)
                        m = pe.matmul(ps[:, j, :], xgT[:, k, :], slot(s)[:, k % 4, :], start=k == 0, stop=k == KD - 1)
                        if k % 4 == 3:
                            m.then_inc(w_used, 1)
                    if j == 0:
                        token_ids(c + 2)
                    else:
                        transpose_act(j - 1)

                def down(b, ks):
                    for k in ks:
                        s = 8 + 2 * b + k // 4
                        if k % 4 == 0:
                            pe.wait_ge(slot_in[s], e16)
                        if k % 2 == 0:
                            pe.wait_ge(actT_ready, c4 + (k // 2 + 1))
                        m = pe.matmul(ps[:, 4 + b, :], actT[:, k, :], slot(s)[:, k % 4, :], start=k == 0, stop=k == KD - 1)
                        if k % 4 == 3:
                            m.then_inc(w_used, 1)

                pe.wait_ge(combined, c2 + 1)
                down(0, range(0, 4))
                transpose_act(3)
                down(0, range(4, 6))
                pe.wait_ge(combined, c2 + 2)
                down(1, range(0, 6))
                down(0, range(6, 8))
                pe.wait_ge(idx_ready, c + 2)
                transpose_x(c * 16 + 32)
                down(1, range(6, 8))

        @block.vector
        def _(dve):
            chain = [0]

            def link(ins):
                chain[0] += 1
                ins.then_inc(dve_step, 1)
                dve.wait_ge(dve_step, chain[0])

            dve.wait_ge(vec_ps, 1)
            link(dve.tensor_copy(vecs[:, 0:NCOL], ps[:, 0, 0:NCOL]))
            dve.memset(vecs[:, C_EPS:C_EPS + 1], EPS)
            lam = col(C_LAM, LT)
            L = [lamt[:, i, :] for i in range(6)]
            link(dve.tensor_scalar(L[0], lam, -1.0, None, ALU.mult))
            dve.tensor_tensor(L[1], L[0], lam, ALU.min).then_inc(lam_in, 1)
            dve.memset(credit[:, 3:4], 0.0).then_inc(vec_ready, 1)
            for n, (a, b) in enumerate(((0, 2), (2, 6), (6, 10))):
                dve.wait_ge(sq_sum, b)
                dve.tensor_scalar(st[:, 16 + a:16 + b], st[:, a:b], 1.0 / D, EPS, ALU.mult, ALU.add).then_inc(ms_ready, 1)
                dve.wait_ge(rt_ready, n + 1)
                link(dve.reciprocal(st[:, 16 + a:16 + b], st[:, 32 + a:32 + b]))
                if n == 2:
                    dve.wait_ge(tr_done, 12)
                for t in range(a, b):
                    if t < 2:
                        m = dve.tensor_scalar(ms[:, t, :], mem_sb[:, t, :], st[:, 16 + t:17 + t], None, ALU.mult)
                    else:
                        m = dve.tensor_scalar(xs[:, (t - 2) % 4, :], xh[:, t - 2, :], st[:, 16 + t:17 + t], None, ALU.mult)
                m.then_inc(scaled, 1)
                if n == 0:
                    for k in range(0, KD, 2):
                        dve.wait_ge(tr_done, k // 2 + 1)
                        for kk in range(2):
                            m = dve.tensor_scalar(memT_v[:, k + kk, :], ps[:, 4 + (k // 2) % 4, kk * MEM:(kk + 1) * MEM],
                                                  col(C_GMEM + k + kk), None, ALU.mult)
                        m.then_inc(tr_out, 1)
                else:
                    h = n - 1
                    for k in range(KD):
                        u = 4 + 8 * h + k
                        dve.wait_ge(tr_done, u + 1)
                        dve.tensor_scalar(xnT[:, k, h * HALF:(h + 1) * HALF], ps[:, 4 + u % 4, :], col(C_GMIX + k), None,
                                          ALU.mult).then_inc(tr_out, 1)
            dve.wait_ge(lam_exp, 1)
            link(dve.tensor_scalar(L[2], L[1], 2.0, None, ALU.add))
            link(dve.reciprocal(L[2], L[2]))
            link(dve.tensor_tensor(L[2], L[1], L[2], ALU.mult))
            link(dve.tensor_tensor(L[3], L[2], L[2], ALU.mult))
            link(dve.tensor_scalar(L[4], L[3], 1.0 / 17, 1.0 / 15, ALU.mult, ALU.add))
            for d in (13, 11, 9, 7, 5, 3, 1):
                link(dve.tensor_tensor(L[4], L[4], L[3], ALU.mult))
                link(dve.tensor_scalar(L[4], L[4], 1.0 / d, None, ALU.add))
            link(dve.scalar_tensor_tensor(out=L[4], in0=L[4], scalar=2.0, in1=L[2], op0=ALU.mult, op1=ALU.mult))
            link(dve.scalar_tensor_tensor(out=L[4], in0=L[0], scalar=0.0, in1=L[4], op0=ALU.max, op1=ALU.add))
            dve.tensor_scalar(col(C_NSP8, LT), L[4], -8.0, None, ALU.mult)
            dve.tensor_scalar(col(C_SP8, LT), L[4], 8.0, None, ALU.mult).then_inc(dve_const, 1)

            for c in range(LT):
                u, xc = uT[:, LRU + c, :], lru_tmp[:, 0, :]
                dve.wait_ge(in_out, upos[(1, LRU + c)] + 1)
                if c == 0:
                    dve.wait_ge(in_done, 12)
                link(dve.tensor_scalar(xc, u, col(C_CONVW + 9 + c), col(C_CONVB + c), ALU.mult, ALU.add))
                for back in (1, 2, 3):
                    m = dve.scalar_tensor_tensor(out=xc[:, back:S], in0=u[:, 0:S - back], scalar=col(C_CONVW + 3 * (3 - back) + c),
                                                 in1=xc[:, back:S], op0=ALU.mult, op1=ALU.add)
                    if back < 3:
                        link(m)
                m.then_inc(conv_done, 1)
                t, w = lru_tmp[:, 3, :], lru_tmp[:, 5, :]
                dve.wait_ge(ab_ready, 2 * c + 1)
                link(dve.tensor_scalar(w, t, 1.0, None, ALU.add))
                link(dve.reciprocal(w, w))
                dve.scalar_tensor_tensor(out=t, in0=t, scalar=2.0, in1=w, op0=ALU.mult, op1=ALU.mult).then_inc(frac_ready, 1)
                ix = lru_tmp[:, 2, :]
                dve.wait_ge(gate_act, 4 * c + 4)
                dve.wait_ge(conv_done, c + 1)
                link(dve.tensor_tensor(ix, ix, xc, ALU.mult))
                dve.wait_ge(root_ready, c + 1)
                link(dve.tensor_tensor(ix, ix, t, ALU.mult))
                dve.wait_ge(ab_ready, 2 * c + 2)
                dve.tensor_tensor_scan(u, lru_tmp[:, 4, :], ix, 0.0, ALU.mult, ALU.add).then_inc(ylru, 1)
                dve.wait_ge(ylru, 2 * c + 1)
                dve.wait_ge(gelu_done, c + 1)
                dve.tensor_tensor(u, u, uT[:, GATE + c, :], ALU.mult).then_inc(ylru, 1)

            for n, (t, w, g) in enumerate(normt):
                dve.wait_ge(nroot, nssc[n + 1])
                r = sqtmp[:, n % 2, 0:w]
                link(dve.reciprocal(r, r))
                dve.scalar_tensor_tensor(out=t, in0=t, scalar=col(g), in1=r, op0=ALU.mult, op1=ALU.mult).then_inc(normed, 1)
            for c in range(LT):
                u = uT[:, LRU + c, :]
                dve.wait_ge(ylru, 2 * c + 2)
                dve.tensor_tensor(lru_tmp[:, 3 + c, :], u, u, ALU.mult).then_inc(lru_sq, 1)
                link(dve.tensor_scalar(u, u, col(C_GOL + c), None, ALU.mult))

            scale = DH ** -0.5
            dve.wait_ge(rt_in, 16 * NRT)
            dve.wait_ge(pool_const, NPOOLC)
            link(dve.tensor_scalar(st[:, 88:94], sinkb[:, :], -1.0, None, ALU.mult))

            def softmax_in(j):
                kind, b = items[j]
                nh = heads(kind)
                sc = scores_sb[:, j % 2, 0:nh, :]
                for k, hs in enumerate(score_banks(kind)):
                    n = len(hs)
                    dve.wait_ge(sc_done, scb[j] + k + 1)
                    if j == 0 and k == 0:
                        dve.wait_ge(in_done, len(units))
                    if j >= 2 and k == 0:
                        dve.wait_ge(pt_done, ytc[j - 1])
                    src = ps[:, k, 0:256 * n].rearrange("p (h k) -> p h k", h=n)
                    dst = scores_sb[:, j % 2, hs[0]:hs[-1] + 1:2, :]
                    if kind == "swa":
                        if b == 0:
                            dve.tensor_copy(dst[:, :, 0:P], band[:, 1:2, 0:P].to_broadcast([P, n, P]))
                            src, dst, mk = src[:, :, P:2 * P], dst[:, :, P:2 * P], band[:, 1:2, P:2 * P].to_broadcast([P, n, P])
                        else:
                            mk = band[:, 0:1, :].to_broadcast([P, n, 2 * P])
                        dve.scalar_tensor_tensor(out=dst, in0=src, scalar=scale, in1=mk,
                                                 op0=ALU.mult, op1=ALU.add).then_inc(sc_out, 1)
                    else:
                        dve.tensor_scalar(dst, src, scale, None, ALU.mult).then_inc(sc_out, 1)
                dve.wait_ge(sc_out, scb[j + 1])
                mx = st[:, 48 + 8 * (j % 2):48 + 8 * (j % 2) + nh]
                link(dve.tensor_reduce(mx, sc, AX_X, ALU.max))
                if kind == "swa":
                    dve.scalar_tensor_tensor(out=mx, in0=mx, scalar=-1.0, in1=st[:, 88:94],
                                             op0=ALU.mult, op1=ALU.min).then_inc(nmx_ready, 1)
                    dve.wait_ge(nmx_ready, j + 1)
                    dve.tensor_tensor(st[:, 80:86], mx, sinkb[:, :], ALU.add).then_inc(sink_in, 1)
                else:
                    dve.tensor_scalar(mx, mx, -1.0, None, ALU.mult).then_inc(nmx_ready, 1)

            def softmax_out(j):
                kind, b = items[j]
                nh = heads(kind)
                sums = st[:, 64 + 8 * (j % 2):64 + 8 * (j % 2) + nh]
                dve.wait_ge(exp_done, hc[j + 1])
                if kind == "swa":
                    dve.wait_ge(sink_exp, b + 1)
                    link(dve.tensor_tensor(sums, sums, st[:, 80:86], ALU.add))
                link(dve.reciprocal(sums, sums))
                dve.wait_ge(pt_done, ytc[j] + 2)
                if j:
                    dve.wait_ge(pv_done, j)
                dve.tensor_copy(probsT[:, 4:8, :], ps[:, 5, :].rearrange("p (a b) -> p a b", a=4)).then_inc(pt_dve, 1)
                dve.wait_ge(pv_done, j + 1)
                if j >= 2:
                    dve.wait_ge(o_ss, j - 1)
                    dve.wait_ge(yt_done, j - 1)
                dve.tensor_tensor(o_sb[:, j % 2, 0:nh * DH].rearrange("p (h d) -> p h d", h=nh),
                                  ps[:, 6, 0:nh * DH].rearrange("p (h d) -> p h d", h=nh),
                                  sums.rearrange("p (h a) -> p h a", a=1).to_broadcast([P, nh, DH]),
                                  ALU.mult).then_inc(o_ready, 1)

            def take_y(j):
                kind, b = items[j]
                dve.wait_ge(yt_done, j + 1)
                base, g = (Q, C_GOS) if kind == "swa" else (QM, C_GOM)
                for t in range(heads(kind) // 2):
                    dve.tensor_scalar(uT[:, base + t, b * P:(b + 1) * P], ps[:, 7, t * P:(t + 1) * P], col(g + t), None,
                                      ALU.mult).then_inc(yt_out, 1)

            for j in range(len(items) + 1):
                if j < len(items):
                    softmax_in(j)
                if j >= 1:
                    softmax_out(j - 1)
                    take_y(j - 1)
            dve.wait_ge(o_ss, len(items))
            dve.wait_ge(lru_ss, 1)
            link(dve.tensor_scalar(grp[:, 0:8], ps[:, 0, 0:NT], 1.0 / DL, EPS, ALU.mult, ALU.add))
            sso = st[:, 96:112].rearrange("p (b two) -> p two b", two=2)
            link(dve.tensor_scalar(grp[:, 8:16], sso[:, 0, :], 1.0 / DL, EPS, ALU.mult, ALU.add))
            dve.tensor_scalar(grp[:, 16:24], sso[:, 1, :], 1.0 / (NM * DH), EPS, ALU.mult, ALU.add).then_inc(grp_ms, 1)
            dve.wait_ge(grp_root, 1)
            link(dve.reciprocal(grp[:, 0:24], grp[:, 0:24]))

            def residual(i):
                for g in range(3):
                    for half in range(2):
                        n = 6 * i + 2 * g + half
                        dve.wait_ge(op_done, n + 1)
                        if g:
                            dve.wait_ge(op_out, n - 1)
                        hh = xh[:, i, half * HALF:(half + 1) * HALF]
                        dve.scalar_tensor_tensor(out=hh, in0=ps[:, 2 * g + half, :], scalar=grp[:, 8 * g + i:8 * g + i + 1],
                                                 in1=hh, op0=ALU.mult, op1=ALU.add).then_inc(op_out, 1)

            def ffn_norm(i):
                dve.wait_ge(h_sq, i + 1)
                dve.tensor_scalar(st[:, 8 + i:9 + i], st[:, i:i + 1], 1.0 / D, EPS, ALU.mult, ALU.add).then_inc(h_ms, 1)
                dve.wait_ge(h_root, i + 1)
                link(dve.reciprocal(st[:, 24 + i:25 + i], st[:, 16 + i:17 + i]))
                if i >= 2:
                    dve.wait_ge(xt_done, 2 * (i - 2) + 2)
                    dve.wait_ge(xrow_out[i % 2], 16 * (i // 2))
                dve.scalar_tensor_tensor(out=xrow[i % 2], in0=xh[:, i, :], scalar=st[:, 24 + i:25 + i], in1=gbc,
                                         op0=ALU.mult, op1=ALU.mult).then_inc(xr_ready, 1)

            def take_logits(i):
                dve.wait_ge(lg_done, i + 1)
                dve.tensor_tensor(lg[:, i, :], ps[:, 7, 0:E], b_rt[:, :], ALU.add).then_inc(lg_out, 1)

            dve.wait_ge(gbc_in, 16)
            for i in range(NT + 1):
                if i < NT:
                    residual(i)
                    ffn_norm(i)
                if i >= 1:
                    take_logits(i - 1)
            dve.wait_ge(lg_out, NT)
            for i in range(NT):
                m = dve.max(top8[:, i, :], lg[:, i, :])
            link(m)
            for i in range(NT):
                m = dve.max_index(idx8[:, i, :], top8[:, i, :], lg[:, i, :])
            link(m)
            dve.tensor_tensor(ex[:, :, :], lg[:, :, :], top8[:, :, 0:1].to_broadcast([P, NT, E]),
                              ALU.subtract).then_inc(ex_in, 1)
            link(dve.tensor_copy(idxf[:, :, :], idx8[:, :, :]))
            ie = iota_e[:, :].rearrange("p (a e) -> p a e", a=1).to_broadcast([P, NT, E])
            link(dve.tensor_tensor(mask[:, :, :], ie, idxf[:, :, 0:1].to_broadcast([P, NT, E]), ALU.is_equal))
            for k in range(1, TOPK):
                link(dve.tensor_tensor(tmpe[:, :, :], ie, idxf[:, :, k:k + 1].to_broadcast([P, NT, E]), ALU.is_equal))
                link(dve.tensor_tensor(mask[:, :, :], mask[:, :, :], tmpe[:, :, :], ALU.add))
            dve.tensor_copy(maskb[:, :, :], mask[:, :, :]).then_inc(mask_ready, 1)
            dve.wait_ge(ex_done, 1)
            link(dve.tensor_tensor(gates[:, :, :], ex[:, :, :], mask[:, :, :], ALU.mult))
            link(dve.tensor_reduce(st[:, 0:NT], gates[:, :, :], AX_X, ALU.add))
            link(dve.reciprocal(st[:, 8:8 + NT], st[:, 0:NT]))
            dve.tensor_tensor(gates[:, :, :], gates[:, :, :],
                              st[:, 8:8 + NT].rearrange("p (t a) -> p t a", a=1).to_broadcast([P, NT, E]),
                              ALU.mult).then_inc(gates_ready, 1)
            dve.wait_ge(pos_done, 1)
            link(dve.scalar_tensor_tensor(out=posm[:, :, :], in0=ps[:, 2, 0:NT * E].rearrange("p (t e) -> p t e", t=NT),
                                          scalar=1.0, in1=mask[:, :, :], op0=ALU.add, op1=ALU.mult))
            link(dve.tensor_scalar(posm[:, :, :], posm[:, :, :], -1.0, None, ALU.add))
            link(dve.tensor_copy(cnt[:, :], ps[:, 3, 0:E]))
            link(dve.tensor_scalar(nchunk[:, :], cnt[:, :], 0.0, None, ALU.is_gt))
            for j in range(1, MAXCH):
                link(dve.scalar_tensor_tensor(out=nchunk[:, :], in0=cnt[:, :], scalar=float(j * P), in1=nchunk[:, :],
                                              op0=ALU.is_gt, op1=ALU.add))
            link(dve.tensor_tensor_scan(cum[:, :], nchunk[:, :], nchunk[:, :], 0.0, ALU.add, ALU.max))
            link(dve.tensor_scalar(tmpe[:, 0, :], cum[:, :], iota_p[:, 0:1], None, ALU.is_le))
            link(dve.tensor_tensor(tmpe[:, 1, :], tmpe[:, 0, :], cum[:, :], ALU.mult))
            link(dve.tensor_reduce(st[:, 16:17], tmpe[:, 0, :], AX_X, ALU.add))
            link(dve.tensor_reduce(st[:, 18:19], tmpe[:, 1, :], AX_X, ALU.max))
            link(dve.tensor_scalar(ctab[:, 0:1], st[:, 16:17], float(E - 1), None, ALU.min))
            link(dve.tensor_tensor(ctab[:, 1:2], iota_p[:, 0:1], st[:, 18:19], ALU.subtract))
            dve.tensor_scalar(ctab[:, 1:2], ctab[:, 1:2], float(MAXCH), None, ALU.min).then_inc(ctab_ready, 1)
            link(dve.tensor_copy(ttab[0:1, 2 * P:2 * P + E], cum[0:1, :]))
            dve.wait_ge(ttab_ps, 1)
            dve.tensor_copy(ttab[0:1, 0:2 * P], ps[0:1, 4, 0:2 * P]).then_inc(ttab_ready, 1)
            for u in range(2 * NT):
                i, half = u // 2, u % 2
                dve.wait_ge(init_mm, u + 1)
                hh = xh[:, i, half * HALF:(half + 1) * HALF]
                dve.tensor_tensor(hh, ps[:, 5 + u % 2, :], hh, ALU.add).then_inc(init_ready, 1)

            dve.wait_ge(ttab_ready, 1)
            dve.wait_ge(zeroed, 3)
            total = dve.value_load(ttab[0:1, 2 * P + E - 1:2 * P + E], min_val=1, max_val=NCH)

            def make_onehot(n):
                e = dve.value_load(ttab[0:1, bass.ds(n, 1)], min_val=0, max_val=E - 1)
                part = dve.value_load(ttab[0:1, bass.ds(n + P, 1)], min_val=0, max_val=MAXCH)
                dve.tensor_tensor(onehot[:, :, :],
                                  iota_s[:, bass.ds(part * P, P)].rearrange("p (a s) -> p a s", a=1).to_broadcast([P, NT, P]),
                                  posm[:, :, bass.ds(e, 1)].to_broadcast([P, NT, P]), ALU.is_equal).then_inc(onehot_ready, 1)

            def make_idx(n):
                dve.wait_ge(ids_done, n)
                dve.tensor_scalar(pad[:, :], ps[:, 6, 0:1], 0.0, float(AHEAD_OOB), ALU.is_equal, ALU.mult).then_inc(moe_step, 1)
                dve.wait_ge(moe_step, n)
                dve.scalar_tensor_tensor(out=idx_next[:, :], in0=ps[:, 6, 0:1], scalar=-1.0, in1=pad[:, :],
                                         op0=ALU.add, op1=ALU.add).then_inc(idx_ready, 1)

            dve.memset(credit[:, 1:2], 0.0).then_inc(h_free, 4)
            dve.memset(credit[:, 2:3], 0.0).then_inc(combined, 2)
            dve.memset(credit[:, 3:4], 0.0).then_inc(w_used, NSLOT)
            make_onehot(0)
            make_idx(1)
            with dve.Fori(0, total) as c:
                e = dve.value_load(ttab[0:1, bass.ds(c, 1)], min_val=0, max_val=E - 1)
                c4 = dve.snap(c * 4)
                c1 = dve.snap(c + 1)
                w0 = dve.snap(c * NSLOT + NSLOT)
                dve.wait_ge(combined, c * 2 + 2)
                dve.wait_ge(xg_in, c * 16 + 16)
                dve.tensor_copy(gate_cur[:, :], xg[:, bass.ds(e + D, 1)]).then_inc(gate_copied, 1)
                make_onehot(c + 1)
                dve.wait_ge(b1_in, e * 16 + 16)
                bias = dve.snap(e % 2 * (2 * FF))

                def glu_piece(j):
                    hj = hb[:, j % 2, :]
                    dve.wait_ge(w_used, w0 + (2 * j + 2))
                    m = dve.tensor_tensor(hj, ps[:, j, :], b1b[:, bass.ds(bias + j * HALF, HALF)], ALU.add)
                    m.then_inc(h_free, 1)
                    dve.wait_ge(h_free, c4 + (5 + j))
                    pair = hj.rearrange("p (n two) -> p two n", two=2)
                    dve.tensor_scalar(glu[:, j % 2, :], pair[:, 0, :], LIMIT, None, ALU.min).then_inc(glu_ready, 1)
                    dve.tensor_scalar(lin[:, j % 2, :], pair[:, 1, :], LIMIT, -LIMIT, ALU.min, ALU.max).then_inc(lin_ready, 1)
                    dve.wait_ge(lin_ready, c4 + (j + 1))
                    dve.scalar_tensor_tensor(out=lin[:, j % 2, :], in0=lin[:, j % 2, :], scalar=1.0, in1=glu[:, j % 2, :],
                                             op0=ALU.add, op1=ALU.mult).then_inc(lin_done, 1)

                def act_piece(j):
                    dve.wait_ge(sig_ready, c4 + (j + 1))
                    dve.wait_ge(lin_done, c4 + (j + 1))
                    if j >= 2:
                        dve.wait_ge(at_done, c4 + (j - 1))
                    dve.tensor_tensor(act[:, j % 2, :], lin[:, j % 2, :], sig[:, j % 2, :], ALU.mult).then_inc(act_ready, 1)

                glu_piece(0)
                act_piece(0)
                dve.wait_ge(idxcur_ready, c + 1)
                make_idx(c + 2)
                for j in range(1, 4):
                    glu_piece(j)
                    act_piece(j)
                dve.wait_ge(rows_in, c * 16 + 16)
                for b in range(2):
                    dve.wait_ge(w_used, w0 + (11 + b))
                    rb = rows[:, b * HALF:(b + 1) * HALF]
                    dve.scalar_tensor_tensor(out=rb, in0=ps[:, 4 + b, :], scalar=gate_cur[:, 0:1], in1=rb,
                                             op0=ALU.mult, op1=ALU.add).then_inc(combined, 1)


_INS = ["x", "mem", "g_mix", "w_in", "conv_w", "conv_b", "lru_wa", "lru_ba", "lru_wx", "lru_bx", "lru_lambda",
        "q_norm_swa", "k_norm_swa", "swa_sinks", "g_mem", "w_mem_kv", "q_norm_mem", "k_norm_mem",
        "g_out_lru", "g_out_swa", "g_out_mem", "w_out", "g_ffn", "w_router", "b_router", "w1", "b1", "w2", "b2"]


def kernel(**inputs):
    import numpy as _np
    import concourse.bacc as _bacc
    from concourse.bass_utils import run_bass_kernel_spmd as _run

    nc = _bacc.Bacc("TRN2", target_bir_lowering=False, num_devices=1)
    arrays, args = {}, []
    for name in _INS:
        a = _np.ascontiguousarray(inputs[name])
        arrays[f"in_{name}"] = a
        args.append(nc.dram_tensor(f"in_{name}", a.shape, mybir.dt.from_np(a.dtype), kind="ExternalInput").ap())
    xrows = nc.dram_tensor("token_rows", (S, XW), F32, kind="Internal").ap()
    out = nc.dram_tensor("out", (1, S, D), F32, kind="ExternalOutput").ap()
    hymba_layer(nc, *args, xrows, out)
    r = _run(nc, [arrays], core_ids=[0])
    return r.results[0]["out"]
```

```python
from contextlib import ExitStack

import concourse.bass as bass
from concourse import mybir

F32 = mybir.dt.float32
F32R = mybir.dt.float32r
F16 = mybir.dt.float16
BF16 = mybir.dt.bfloat16
I32 = mybir.dt.int32
U32 = mybir.dt.uint32
ALU = mybir.AluOpType
ACT = mybir.ActivationFunctionType
AX_X = mybir.AxisListType.X

P = 128
D = 1024
S = 1024
NT = S // P
KD = D // P
MEM = 256
DH = 64
NQ = 6
NM = 4
DL = 384
LT = DL // P
E = 32
TOPK = 4
FF = 1024
HALF = 512
EPS = 1e-6
LIMIT = 7.0
ALPHA = 1.702
PASS = 2 * P
MAXPART = S // PASS
NPASS = 50
XW = D + E
SLOT = 2048
NSLOT = 12
RAW = 6
SPLIT = 4
LEAD = 3
BY_POOL = (7, 11)
AHEAD_OOB = 1 << 20

LRU, GATE, Q, K, V, QM = 0, 3, 6, 9, 10, 11
NCT = 13
C_GMIX, C_GMEM, C_CONVW, C_CONVB, C_BA, C_BX, C_LAM, C_QS, C_KS, C_QM, C_KM, C_GOL, C_GOS, C_GOM = (
    0, 8, 16, 28, 31, 34, 37, 40, 41, 42, 43, 44, 47, 50)
NCOL = 52
C_EPS, C_SP8, C_NSP8 = 52, 53, 56
NVEC = 10 + 8
NPOOLC = 11
NRT = 3


def hymba_layer(nc, x, mem, g_mix, w_in, conv_w, conv_b, lru_wa, lru_ba, lru_wx, lru_bx, lru_lambda,
                q_norm_swa, k_norm_swa, swa_sinks, g_mem, w_mem_kv, q_norm_mem, k_norm_mem,
                g_out_lru, g_out_swa, g_out_mem, w_out, g_ffn, w_router, b_router, w1, b1, w2, b2,
                xrows, out):
    with ExitStack() as ctx:
        def sb(name, shape, dt=F32):
            return ctx.enter_context(nc.sbuf_tensor(name, shape, dt))

        def sem(name):
            return ctx.enter_context(nc.semaphore(name))

        ring = sb("ring", [P, RAW * SLOT])
        km = sb("km", [P, 2, MEM])
        vm = sb("vm", [P, 2, MEM])
        ident = sb("ident", [P, P])
        st = sb("st", [P, 128])
        maskb = sb("maskb", [P, NT, E], BF16)
        top8 = sb("top8", [P, NT, 8])
        idx8 = sb("idx8", [P, NT, 8], U32)
        idxf = sb("idxf", [P, NT, 8])
        iota_e = sb("iota_e", [P, E])
        iota_p = sb("iota_p", [P, 1])
        tri = sb("tri", [P, P], BF16)
        onesb = sb("onesb", [P, P], BF16)
        tokid = sb("tokid", [P, NT], F16)
        cnt = sb("cnt", [P, E])
        npass = sb("npass", [P, E])
        cum = sb("cum", [P, E])
        ptab = sb("ptab", [P, 3])
        TE, TPART, TTWO, TDBL, TALL = 0, P, 2 * P, 3 * P, 4 * P
        ttab = sb("ttab", [1, 4 * P + 1], I32)
        dblrow = sb("dblrow", [1, 2 * P])
        credit = sb("credit", [P, 16])
        idx_next = sb("idx_next", [P, 2], I32)
        idx_cur = sb("idx_cur", [P, 2], I32)
        no_index = sb("no_index", [P, 2], I32)
        pad = sb("pad", [P, 2])
        gate_cur = sb("gate_cur", [P, 2])

        early = ExitStack()

        def sb_early(name, shape, dt=F32):
            return early.enter_context(nc.sbuf_tensor(name, shape, dt))
        work = sb_early("work", [P, 14336])
        uT = sb_early("uT", [P, NCT, S])
        xh = sb_early("xh", [P, NT, D])

        wB = ring[:, 0:7168].rearrange("p (k c) -> p k c", k=KD)
        mem_sb = ring[:, 7168:9216].rearrange("p (t d) -> p t d", t=2)
        sqtmp = ring[:, 9216:11264].rearrange("p (i t) -> p i t", i=2)
        band = ring[:, 11264:11776].rearrange("p (i k) -> p i k", i=2)
        wA = work[:, 0:6144].rearrange("p (k c) -> p k c", k=KD)
        xnT = work[:, 6144:14336].rearrange("p (k t) -> p k t", k=KD)
        w_out_sb = work[:, 6144:14336].rearrange("p (k c) -> p k c", k=KD)
        lru_tmp = work[:, 0:6144].rearrange("p (i t) -> p i t", i=6)
        scores_sb = ring[:, 0:4608].rearrange("p (b h k) -> p b h k", b=3, h=NQ)
        probsT = ring[:, 4608:6144].rearrange("p (j q) -> p j q", j=12)
        o_sb = ring[:, 6144:6912].rearrange("p (b c) -> p b c", b=2)
        o_sq = ring[:, 11776:12160]
        xs = uT[:, 5:9, :]
        w_mem = uT[:, 9:13, :].rearrange("p a b -> p (a b)").rearrange("p (k c) -> p k c", k=KD)
        ms = uT[:, 3:5, :]
        sqscr = uT[:, 0, :]
        memT_v = uT[:, 1:3, :].rearrange("p a b -> p (a b)").rearrange("p (k t) -> p k t", k=KD)
        kz = [[ring[:, 7168 + g * S:7168 + (g + 1) * S], lru_tmp[:, 2 * g, :]] for g in range(2)]
        kmz = lru_tmp[:, 1, :].rearrange("p (h m) -> p h m", h=NM)

        ones = sb_early("ones", [P, P])
        NH = 14
        headcol = sb_early("headcol", [P, 2 * NH])
        headrow = ring[:, 6144:7040].rearrange("p (a b) -> p a b", a=NH)
        rroot = ring[:, 4608:5632]
        gate_w = sb_early("gate_w", [P, 2, LT, P])
        w_rt = sb_early("w_rt", [P, KD, E])
        b_rt = sb_early("b_rt", [P, E])
        sinkb = sb_early("sinkb", [P, NQ])
        vecs = sb_early("vecs", [P, 64])
        vrow = sb_early("vrow", [NCOL, P])

        def col(i, n=1):
            return vecs[:, i:i + n]
        lamt = sb_early("lamt", [P, 6, LT])

        grp = sb_early("grp", [P, 24])

        nmx, row_sums = ([st[:, base + 8 * i:base + 8 * (i + 1)] for i in range(3)] for base in (0, 24))
        sinkx = [st[:, 48 + 8 * i:54 + 8 * i] for i in range(2)]

        uflat = uT[:, :, :].rearrange("p a b -> p (a b)")
        xrow = [uT[:, GATE + i, :] for i in range(2)]
        gbc = uT[:, GATE + 2, :]
        xrT = [uT[:, 9 + i, :].rearrange("p (k t) -> p k t", k=KD) for i in range(2)]

        lg, ex, mask, tmpe = (sqtmp[:, 1, i * NT * E:(i + 1) * NT * E].rearrange("p (t e) -> p t e", t=NT)
                              for i in range(4))
        gates, posm = (a[:, :, :].rearrange("p a b -> p (a b)")[:, 0:NT * E].rearrange("p (t e) -> p t e", t=NT)
                       for a in (km, vm))
        gatesT, b2_sb = uT[:, 11, :], uT[:, 12, :]


        early.close()
        w_hi = [sb(f"w_hi{i}", [P, 4, HALF], F32R) for i in range(SPLIT)]
        w_lo = [sb(f"w_lo{i}", [P, 4, HALF], F32R) for i in range(SPLIT)]
        xg = sb("xg", [P, 2, XW])
        onehot = sb("onehot", [P, NT, PASS], F16)
        iota_s = sb("iota_s", [P, S + PASS])
        xT_hi, xT_lo, actT_hi, actT_lo = ([sb(f"{n}{g}", [P, KD, P], F32R) for g in range(2)]
                                          for n in ("xT_hi", "xT_lo", "actT_hi", "actT_lo"))
        hb = sb("hb", [P, 2, HALF])
        glu, lin, sig, act = (sb(n, [P, 2, 2, HALF // 2]) for n in ("glu", "lin", "sig", "act"))
        rows = sb("rows", [P, 2, D])
        b1b = sb("b1b", [P, 2 * FF])

        ps = ctx.enter_context(nc.psum_tensor("ps", [P, 8, HALF], F32))

        mem_in, w_mem_in, vec_in, rt_in, wout_in, kz_in, b2_in, gbc_in = map(
            sem, "mem_in w_mem_in vec_in rt_in wout_in kz_in b2_in gbc_in".split())
        x_in = [sem(f"x_in{i}") for i in range(2)]
        wA_in = [sem(f"wA_in{i}") for i in range(2)]
        wB_in = [sem(f"wB_in{i}") for i in range(3)]
        xrow_out = [sem(f"xrow_out{i}") for i in range(2)]
        gates_out, init_out = sem("gates_out"), sem("init_out")
        pool_const = sem("pool_const")
        dve_const = sem("dve_const")
        pool_step, dve_step = sem("pool_step"), sem("dve_step")
        sq_sum = sem("sq_sum")
        ms_ready = sem("ms_ready")
        rt_ready = sem("rt_ready")
        scaled = sem("scaled")
        tr_done, tr_out = sem("tr_done"), sem("tr_out")
        mkv_done, mkv_out = sem("mkv_done"), sem("mkv_out")
        in_done, in_out = sem("in_done"), sem("in_out")
        conv_done = sem("conv_done")
        gate_mm, gate_act = sem("gate_mm"), sem("gate_act")
        ab_ready, frac_ready, root_ready = sem("ab_ready"), sem("frac_ready"), sem("root_ready")
        gelu_done, ylru, lru_sq, lru_ss = sem("gelu_done"), sem("ylru"), sem("lru_sq"), sem("lru_ss")
        nsq, nss, nroot, normed = sem("nsq"), sem("nss"), sem("nroot"), sem("normed")
        sc_done, sc_out, nmx_ready, exp_done, sink_in, sink_exp = map(
            sem, "sc_done sc_out nmx_ready exp_done sink_in sink_exp".split())
        pt_done, pt_act, pt_dve, pv_done, o_ready, o_ss, yt_done, yt_out = map(
            sem, "pt_done pt_act pt_dve pv_done o_ready o_ss yt_done yt_out".split())
        grp_ms, grp_root, grp_rs = sem("grp_ms"), sem("grp_root"), sem("grp_rs")
        op_done, op_out, h_sq, h_ms, h_root, xr_ready = map(
            sem, "op_done op_out h_sq h_ms h_root xr_ready".split())
        xt_done, xt_out, lg_done, lg_out = map(sem, "xt_done xt_out lg_done lg_out".split())
        ex_in, ex_done, mask_ready, pos_done, gates_ready, gt_done, gt_out, init_mm, init_ready = map(
            sem, "ex_in ex_done mask_ready pos_done gates_ready gt_done gt_out init_mm init_ready".split())
        ptab_ready, ttab_ps, ttab_ready = sem("ptab_ready"), sem("ttab_ps"), sem("ttab_ready")
        slot_in = [sem(f"slot_in{i}") for i in range(RAW)]
        hi_ready = sem("hi_ready")
        lo_ready, lo_pool = sem("lo_ready"), sem("lo_pool")
        w_used, b1_in = sem("w_used"), sem("b1_in")
        onehot_ready, ids_done, idx_ready, idxcur_ready, gate_copied = map(
            sem, "onehot_ready ids_done idx_ready idxcur_ready gate_copied".split())
        xg_in, xgt_done, xhi_ready, xlo_ready = map(sem, "xg_in xgt_done xhi_ready xlo_ready".split())
        (rows_in, scattered, h_free, glu_ready, lin_ready, lin_done, sig_ready, act_ready, at_done,
         ahi_ready, alo_ready, combined) = (
            [sem(f"{n}{g}") for g in range(2)] for n in
            ("rows_in scattered h_free glu_ready lin_ready lin_done sig_ready act_ready at_done "
             "ahi_ready alo_ready combined").split())
        vec_ps, vec_ready, lam_in, lam_exp, gw_in, rroot_ready, spread, lru_gained, kz_zero, padded = map(
            sem, "vec_ps vec_ready lam_in lam_exp gw_in rroot_ready spread lru_gained kz_zero padded".split())
        zeroed, moe_step = sem("zeroed"), sem("moe_step")

        units = [(h, c) for h in range(2) for c in range(6)]
        units += [(h, c) for c in (K, V) for h in range(2)] + [(h, c) for c in (Q, Q + 1, Q + 2, QM, QM + 1) for h in range(2)]
        upos = {u: i for i, u in enumerate(units)}
        normt = [(uT[:, K, :], S, C_KS), (km[:, :, :].rearrange("p a b -> p (a b)"), 2 * MEM, C_KM)]
        normt += [(uT[:, Q + i, :], S, C_QS) for i in range(3)] + [(uT[:, QM + i, :], S, C_QM) for i in range(2)]
        norm_units = [(h, n) for h in range(2) for n, (_, w, _) in enumerate(normt) if h < w // HALF]
        items = [(kind, b) for b in range(NT) for kind in ("swa", "mem")]

        def heads(kind):
            return NQ if kind == "swa" else NM

        def score_banks(kind):
            return [(h, h + 1) for h in range(0, heads(kind), 2)]

        scb, hc, ytc = [0], [0], [0]
        for kind, _ in items:
            scb.append(scb[-1] + len(score_banks(kind)))
            hc.append(hc[-1] + heads(kind))
            ytc.append(ytc[-1] + heads(kind) // 2)
        ptac = [0]
        for kind, _ in items:
            ptac.append(ptac[-1] + (heads(kind) // 2 + 1) // 2)

        def split_before(s, by_pool):
            return sum((i % NSLOT in BY_POOL) == by_pool for i in range(s + 1))

        def slot(s):
            return ring[:, (s % RAW) * SLOT:(s % RAW + 1) * SLOT].rearrange("p (k c) -> p k c", k=4)

        vector_rows = [(base, k, 0, P, v[0].rearrange("(k p) -> k p", p=P)) for base, v, k in (
            (C_GMIX, g_mix, KD), (C_GMEM, g_mem, KD), (C_CONVB, conv_b, LT), (C_BA, lru_ba, LT), (C_BX, lru_bx, LT),
            (C_LAM, lru_lambda, LT), (C_GOL, g_out_lru, LT), (C_GOS, g_out_swa, LT), (C_GOM, g_out_mem, 2))]
        vector_rows += [(C_CONVW, 12, 0, P, conv_w[0].rearrange("w (k p) -> (w k) p", p=P))]
        vector_rows += [(base, 1, half * DH, DH, v) for base, v in (
            (C_QS, q_norm_swa), (C_KS, k_norm_swa), (C_QM, q_norm_mem), (C_KM, k_norm_mem)) for half in range(2)]
        assert len(vector_rows) == NVEC

        def load_vectors(eng, which):
            for base, k, at, n, src in vector_rows[which::2]:
                eng.dma_start(vrow[base:base + k, at:at + n], src).then_inc(vec_in, 16)

        block = ctx.enter_context(nc.Block())

        @block.sync
        def _(sp):
            load_vectors(sp, 0)
            sp.dma_start(mem_sb, mem[0].rearrange("(t p) d -> p t d", p=P)).then_inc(mem_in, 16)
            xv = x[0].rearrange("(t p) d -> p t d", p=P)
            sp.dma_start(xh[:, 0:4, :], xv[:, 0:4, :]).then_inc(x_in[0], 16)
            sp.dma_start(w_mem, w_mem_kv[0].rearrange("(k p) c -> p k c", p=P)).then_inc(w_mem_in, 16)
            sp.dma_start(xh[:, 4:8, :], xv[:, 4:8, :]).then_inc(x_in[1], 16)
            wv = w_in[0].rearrange("(k p) c -> p k c", p=P)
            for i in range(2):
                sp.dma_start(wA[:, :, i * DL:(i + 1) * DL], wv[:, :, i * DL:(i + 1) * DL]).then_inc(wA_in[i], 16)
            for i, (a, b) in enumerate(((384, 640), (0, 384), (640, 896))):
                sp.dma_start(wB[:, :, a:b], wv[:, :, 768 + a:768 + b]).then_inc(wB_in[i], 16)
            sp.wait_ge(in_done, len(units))
            sp.dma_start(w_out_sb, w_out[0].rearrange("(k p) c -> p k c", p=P)).then_inc(wout_in, 16)
            sp.wait_ge(normed, norm_units.index((1, 0)) + 1)
            sp.wait_ge(kz_zero, 5)
            for g in range(2):
                for half in range(2):
                    sp.dma_start(kz[g][half][half * DH:(half + 1) * DH, :],
                                 uT[g * DH:(g + 1) * DH, K, :]).then_inc(kz_in, 16)

            w1v = w1[0].rearrange("e (k p) c -> e p k c", p=P)
            w2v = w2[0].rearrange("e (k p) c -> e p k c", p=P)

            def load_slot(e, s):
                if s < 8:
                    src = w1v[bass.ds(e, 1), :, 4 * (s % 2):4 * (s % 2) + 4, HALF * (s // 2):HALF * (s // 2) + HALF]
                else:
                    kh, b = (s - 8) // 2, s % 2
                    src = w2v[bass.ds(e, 1), :, 4 * kh:4 * kh + 4, HALF * b:HALF * b + HALF]
                sp.dma_start(slot(s), src.rearrange("o p k c -> (o p) k c")).then_inc(slot_in[s % RAW], 16)

            sp.wait_ge(ylru, 2 * LT)
            sp.dma_start(gbc, g_ffn.to_broadcast([P, D])).then_inc(gbc_in, 16)
            sp.wait_ge(lru_ss, 1)
            sp.wait_ge(yt_out, ytc[-1])
            sp.wait_ge(o_ss, len(items))
            for s in range(4):
                load_slot(0, s)
            sp.wait_ge(op_done, 6 * NT)
            sp.wait_ge(padded, 2)
            sp.dma_start(b2_sb[0:E, :], b2[0]).then_inc(b2_in, 16)
            sp.wait_ge(ttab_ready, 1)
            for s in range(4, RAW):
                load_slot(0, s)
            for i in range(NT):
                sp.wait_ge(init_ready, 2 * i + 2)
                sp.dma_start(out[0, i * P:(i + 1) * P, :], xh[:, i, :]).then_inc(init_out, 16)
            sp.wait_ge(init_out, 16 * NT)
            sp.dma_start(b1b[:, :], b1[0, 0:1, :].to_broadcast([P, 2 * FF])).then_inc(b1_in, 16)
            total = sp.value_load(ttab[0:1, TALL:TALL + 1], min_val=1, max_val=NPASS)
            split_reg, pool_reg, hfa_reg, hfb_reg = (sp.alloc_register(n) for n in ("split", "pool", "hfa", "hfb"))
            with sp.Fori(0, total) as p:
                e_now = sp.value_load(ttab[0:1, bass.ds(p + TE, 1)], min_val=0, max_val=E - 1)
                e_next = sp.value_load(ttab[0:1, bass.ds(p + (TE + 1), 1)], min_val=0, max_val=E - 1)
                doubles = sp.value_load(ttab[0:1, bass.ds(p + (TDBL + 1), 1)], min_val=0, max_val=NPASS)
                sp.reg_mul(split_reg, p, NSLOT - len(BY_POOL))
                sp.reg_mul(pool_reg, p, len(BY_POOL))
                for s in range(RAW, RAW + NSLOT):
                    if (s - RAW) % NSLOT in BY_POOL:
                        sp.reg_add(pool_reg, pool_reg, 1)
                        sp.wait_ge(lo_pool, sp.snap(pool_reg))
                    else:
                        sp.reg_add(split_reg, split_reg, 1)
                        sp.wait_ge(lo_ready, sp.snap(split_reg))
                    load_slot(e_now if s < NSLOT else e_next, s % NSLOT)
                sp.reg_mul(hfa_reg, p, 4)
                sp.reg_add(hfa_reg, hfa_reg, 6)
                sp.reg_mul(hfb_reg, doubles, 4)
                sp.reg_add(hfb_reg, hfb_reg, 2)
                hfa, hfb = sp.snap(hfa_reg), sp.snap(hfb_reg)
                sp.wait_ge(h_free[0], hfa)
                sp.wait_ge(h_free[1], hfb)
                sp.dma_start(b1b[:, :], b1[0, bass.ds(e_next, 1), :].to_broadcast([P, 2 * FF])).then_inc(b1_in, 16)
        @block.gpsimd
        def _(po):
            po.memset(ident[:, :], 0.0).then_inc(pool_step, 1)
            po.memset(ones[:, :], 1.0).then_inc(pool_step, 1)
            po.memset(headcol[:, :], 0.0).then_inc(pool_step, 1)
            po.memset(band[:, :, :], 0.0).then_inc(pool_step, 1)
            po.memset(onesb[:, :], 1.0).then_inc(pool_step, 1)
            po.memset(gate_w[:, :, :, :], 0.0).then_inc(pool_step, 1)
            po.wait_ge(pool_step, 6)
            po.affine_select(out=ident[:, :], in_=ident[:, :], compare_op=ALU.not_equal, fill=1.0, base=0,
                             pattern=[[-1, P]], channel_multiplier=1).then_inc(pool_const, 1)
            for half in range(2):
                po.wait_ge(pool_const, half + 1)
                po.memset(headcol[half * DH:(half + 1) * DH, NH + half:NH + half + 1], 1.0).then_inc(pool_const, 1)
            po.wait_ge(pool_const, 3)
            po.affine_select(out=band[:, :, P:2 * P], in_=band[:, :, P:2 * P], compare_op=ALU.is_ge, fill=-1e30,
                             base=0, pattern=[[0, 2], [-1, P]], channel_multiplier=1).then_inc(pool_const, 1)
            po.affine_select(out=band[:, 0, 0:P], in_=band[:, 0, 0:P], compare_op=ALU.is_gt, fill=-1e30,
                             base=0, pattern=[[1, P]], channel_multiplier=-1).then_inc(pool_const, 1)
            po.memset(band[:, 1, 0:P], -1e30).then_inc(pool_const, 1)
            po.affine_select(out=tri[:, :], in_=onesb[:, :], compare_op=ALU.is_gt, fill=0.0, base=0,
                             pattern=[[1, P]], channel_multiplier=-1).then_inc(pool_const, 1)
            po.iota(iota_e[:, :], [[1, E]], base=0, channel_multiplier=0,
                    allow_small_or_imprecise_dtypes=True).then_inc(pool_const, 1)
            po.iota(iota_p[:, :], [[0, 1]], base=0, channel_multiplier=1,
                    allow_small_or_imprecise_dtypes=True).then_inc(pool_const, 1)
            po.iota(tokid[:, :], [[P, NT]], base=1, channel_multiplier=1,
                    allow_small_or_imprecise_dtypes=True).then_inc(pool_const, 1)
            for g, w in enumerate((lru_wa, lru_wx)):
                for half in range(2):
                    po.dma_start(gate_w[half * DH:(half + 1) * DH, g, :, half * DH:(half + 1) * DH],
                                 w[0, half::2].rearrange("h i j -> i h j")).then_inc(gw_in, 16)
            po.dma_start(b_rt[:, :], b_router.to_broadcast([P, E])).then_inc(rt_in, 16)
            po.dma_start(sinkb[:, :], swa_sinks.to_broadcast([P, NQ])).then_inc(rt_in, 16)
            po.dma_start(w_rt[:, :, :], w_router[0].rearrange("(k p) c -> p k c", p=P)).then_inc(rt_in, 16)

            po.wait_ge(in_done, len(units))
            po.memset(rroot, 1.0).then_inc(pool_step, 1)
            po.memset(headrow[:, :, :], 0.0).then_inc(pool_step, 1)
            po.wait_ge(pool_step, 8)
            po.affine_select(out=headrow[:, :, :], in_=headrow[:, :, :], compare_op=ALU.not_equal, fill=1.0, base=0,
                             pattern=[[-1, NH], [0, DH]], channel_multiplier=1).then_inc(pool_const, 1)

            po.memset(kz[0][0], 0.0).then_inc(kz_zero, 1)
            po.memset(kz[1][0], 0.0).then_inc(kz_zero, 1)
            po.wait_ge(ylru, 2 * LT)
            po.memset(kz[0][1], 0.0).then_inc(kz_zero, 1)
            po.memset(kz[1][1], 0.0).then_inc(kz_zero, 1)
            po.memset(kmz[:, :, :], 0.0).then_inc(kz_zero, 1)
            for c in range(LT):
                u = uT[:, LRU + c, :]
                po.wait_ge(ylru, 2 * c + 2)
                if c == 0:
                    po.wait_ge(ylru, 2 * LT)
                po.tensor_tensor(lru_tmp[:, 3 + c, :], u, u, ALU.mult).then_inc(lru_sq, 1)
                po.wait_ge(lru_sq, c + 1)
                po.tensor_scalar(u, u, col(C_GOL + c), None, ALU.mult).then_inc(lru_gained, 1)

            for i in range(NT):
                po.wait_ge(xr_ready, i + 1)
                po.dma_start(xrows[i * P:(i + 1) * P, 0:D], xrow[i % 2]).then_inc(xrow_out[i % 2], 16)

            for i in range(2):
                po.wait_ge(xrow_out[i], 16 * NT // 2)
            po.wait_ge(op_done, 6 * NT)
            po.wait_ge(xt_done, 2 * NT)
            po.memset(gatesT, 0.0).then_inc(padded, 1)
            po.memset(b2_sb, 0.0).then_inc(padded, 1)
            po.memset(xg[:, :, :], 0.0).then_inc(zeroed, 1)
            po.iota(iota_s[:, :], [[1, S + PASS]], base=0, channel_multiplier=0,
                    allow_small_or_imprecise_dtypes=True).then_inc(zeroed, 1)
            po.wait_ge(gates_ready, 1)
            po.dma_start(xrows.rearrange("(t p) c -> p t c", p=P)[:, :, D:XW], gates[:, :, :]).then_inc(gates_out, 16)
            po.wait_ge(gates_out, 16)

            none_reg, last_row = po.alloc_register("none"), po.alloc_register("last_row")
            po.reg_mov(none_reg, 0)

            def by_index(idx, g):
                return bass.IndirectOffsetOnAxis(ap=idx[:, g:g + 1], axis=0)

            def gather_x():
                po.wait_ge(zeroed, 2)
                for g in range(2):
                    po.reg_add(last_row, none_reg, S - 1)
                    po.indirect_dma_start(out=xg[:, g, :], out_offset=None, in_=xrows[:, :],
                                          in_offset=by_index(idx_next, g),
                                          bounds_check=last_row, oob_is_err=False).then_inc(xg_in, 16)

            po.wait_ge(idx_ready, 1)
            gather_x()
            po.wait_ge(init_out, 16 * NT)
            po.memset(rows[:, :, :], 0.0).then_inc(zeroed, 1)
            po.memset(no_index[:, :], 0).then_inc(zeroed, 1)
            po.wait_ge(zeroed, 4)
            total = po.value_load(ttab[0:1, TALL:TALL + 1], min_val=1, max_val=NPASS)
            with po.Fori(0, total) as p:
                two = po.value_load(ttab[0:1, bass.ds(p + TTWO, 1)], min_val=0, max_val=1)
                dbl = po.value_load(ttab[0:1, bass.ds(p + TDBL, 1)], min_val=0, max_val=NPASS)

                p12 = po.snap(p * NSLOT)
                before = (p, dbl)

                def body(groups):
                    def split_lo(s):
                        po.wait_ge(hi_ready, p12 + (s + 1))
                        po.tensor_tensor(w_lo[s % SPLIT][:, :, :], slot(s), w_hi[s % SPLIT][:, :, :].bitcast(F32),
                                         ALU.subtract).then_inc(lo_pool, 1)

                    po.tensor_tensor(idx_cur[:, :], idx_next[:, :], no_index[:, :], ALU.add).then_inc(idxcur_ready, 1)
                    po.wait_ge(idx_ready, p + 2)
                    po.wait_ge(xgt_done, p * 2 + 2)
                    po.wait_ge(gate_copied, p + 1)
                    gather_x()
                    po.wait_ge(idxcur_ready, p + 1)
                    for g in groups:
                        po.reg_add(last_row, none_reg, S - 1)
                        po.indirect_dma_start(out=rows[:, g, :], out_offset=None, in_=out[0],
                                              in_offset=by_index(idx_cur, g),
                                              bounds_check=last_row, oob_is_err=False).then_inc(rows_in[g], 16)
                    for s in BY_POOL:
                        split_lo(s)
                    for g in groups:
                        po.wait_ge(combined[g], before[g] * 2 + 4)
                        po.reg_add(last_row, none_reg, S - 1)
                        po.indirect_dma_start(out=out[0], out_offset=by_index(idx_cur, g), in_=rows[:, g, :],
                                              in_offset=None, bounds_check=last_row,
                                              oob_is_err=False).then_inc(scattered[g], 16)
                    for g in groups:
                        po.wait_ge(scattered[g], before[g] * 16 + 16)

                with po.If(two > 0):
                    body((0, 1))
                with po.Else():
                    body((0,))
            po.wait_ge(xg_in, total * 32 + 32)

        @block.scalar
        def _(act_e):
            load_vectors(act_e, 1)
            def root_of_mean(n):
                a, b = ((0, 2), (2, 6), (6, 10))[n]
                act_e.wait_ge(ms_ready, n + 1)
                act_e.activation(st[:, 32 + a:32 + b], st[:, 16 + a:16 + b], ACT.Sqrt).then_inc(rt_ready, 1)

            act_e.wait_ge(mem_in, 16)
            for t in range(2):
                if t:
                    act_e.wait_ge(sq_sum, 1)
                act_e.activation(sqscr, mem_sb[:, t, :], ACT.Square, accum_out=st[:, t:t + 1]).then_inc(sq_sum, 1)
            root_of_mean(0)
            act_e.wait_ge(lam_in, 1)
            act_e.activation(lamt[:, 1, :], lamt[:, 1, :], ACT.Exp).then_inc(lam_exp, 1)
            for h in range(2):
                act_e.wait_ge(x_in[h], 16)
                for t in range(4):
                    i = 4 * h + t
                    act_e.wait_ge(sq_sum, i + 2)
                    act_e.activation(sqscr, xh[:, i, :], ACT.Square,
                                     accum_out=st[:, 2 + i:3 + i]).then_inc(sq_sum, 1)
                root_of_mean(1 + h)
            for u in range(4):
                act_e.wait_ge(mkv_done, u + 1)
                dst = km[:, u, :] if u < 2 else vm[:, u - 2, :]
                act_e.activation(dst, ps[:, u, 0:MEM], ACT.Copy).then_inc(mkv_out, 1)

            def take_unit(i):
                h, c = units[i]
                act_e.wait_ge(in_done, i + 1)
                if i == 0:
                    act_e.wait_ge(sq_sum, 10)
                act_e.activation(uT[:, c, h * HALF:(h + 1) * HALF], ps[:, i % 4, :], ACT.Copy).then_inc(in_out, 1)

            def lru_gates(c):
                for g, bias in ((0, C_BA), (1, C_BX)):
                    for h in range(2):
                        act_e.wait_ge(gate_mm, 4 * c + 2 * g + h + 1)
                        if c and g == 0 and h == 0:
                            act_e.wait_ge(ylru, 2 * c)
                        act_e.activation(lru_tmp[:, 1 + g, h * HALF:(h + 1) * HALF], ps[:, 4 + 2 * g + h, :], ACT.Sigmoid,
                                         bias=col(bias + c)).then_inc(gate_act, 1)
                act_e.wait_ge(gate_act, 4 * c + 2)
                act_e.activation(lru_tmp[:, 3, :], lru_tmp[:, 1, :], ACT.Tanh, scale=col(C_SP8 + c)).then_inc(ab_ready, 1)
                act_e.activation(lru_tmp[:, 4, :], lru_tmp[:, 1, :], ACT.Exp, scale=col(C_NSP8 + c)).then_inc(ab_ready, 1)
                act_e.wait_ge(frac_ready, c + 1)
                act_e.activation(lru_tmp[:, 3, :], lru_tmp[:, 3, :], ACT.Sqrt).then_inc(root_ready, 1)
                act_e.wait_ge(in_out, upos[(1, GATE + c)] + 1)
                act_e.activation(uT[:, GATE + c, :], uT[:, GATE + c, :], ACT.Gelu_apprx_tanh).then_inc(gelu_done, 1)

            nA = 12
            for i in range(nA):
                take_unit(i)
            act_e.wait_ge(dve_const, 1)
            left = list(range(nA, len(units)))
            for c in range(LT):
                for i in left[5 * c:5 * c + 5]:
                    take_unit(i)
                lru_gates(c)
            assert not left[15:]

            for n, (t, w, g) in enumerate(normt):
                if n == 0:
                    act_e.wait_ge(mkv_out, 4)
                    act_e.wait_ge(in_out, len(units))
                if n >= 2:
                    act_e.wait_ge(nss, n - 1)
                act_e.activation(sqtmp[:, n % 2, 0:w], t, ACT.Square).then_inc(nsq, 1)
            for h in range(2):
                act_e.wait_ge(nss, len(normt))
                act_e.activation(rroot[0:NH, h * HALF:(h + 1) * HALF], ps[0:NH, 4 + h, :],
                                 ACT.Sqrt, bias=col(C_EPS)[0:NH], scale=1.0 / DH).then_inc(nroot, 1)

            def exps(j):
                kind, b = items[j]
                nh = heads(kind)
                act_e.wait_ge(nmx_ready, j + 1)
                if j >= 3:
                    act_e.wait_ge(o_ready, j - 2)
                for h in range(nh):
                    act_e.activation(scores_sb[:, j % 3, h, :], scores_sb[:, j % 3, h, :], ACT.Exp,
                                     bias=nmx[j % 3][:, h:h + 1],
                                     accum_out=row_sums[j % 3][:, h:h + 1]).then_inc(exp_done, 1)
                if kind == "swa":
                    act_e.wait_ge(sink_in, b + 1)
                    act_e.activation(sinkx[b % 2], sinkx[b % 2], ACT.Exp).then_inc(sink_exp, 1)

            def take_probs(j):
                kind, b = items[j]
                for k in range(0, heads(kind) // 2, 2):
                    act_e.wait_ge(pt_done, ytc[j] + k + 1)
                    if j:
                        act_e.wait_ge(pv_done, j)
                    act_e.activation(probsT[:, 4 * k:4 * k + 4, :], ps[:, 4, :].rearrange("p (a b) -> p a b", a=4),
                                     ACT.Copy).then_inc(pt_act, 1)

            def take_o(j):
                kind, b = items[j]
                w = heads(kind) * DH
                act_e.wait_ge(o_ready, j + 1)
                if j:
                    act_e.wait_ge(o_ss, j)
                act_e.activation(o_sq[:, 0:w], o_sb[:, j % 2, 0:w], ACT.Square,
                                 accum_out=st[:, 96 + j:97 + j]).then_inc(o_ss, 1)

            exps(0)
            exps(1)
            for j in range(len(items)):
                take_probs(j)
                if j:
                    take_o(j - 1)
                if j + 2 < len(items):
                    exps(j + 2)
            take_o(len(items) - 1)
            act_e.wait_ge(grp_ms, 1)
            act_e.activation(grp[:, 0:24], grp[:, 0:24], ACT.Sqrt).then_inc(grp_root, 1)
            for i in range(NT):
                act_e.wait_ge(op_out, 6 * i + 6)
                if i:
                    act_e.wait_ge(h_sq, i)
                act_e.activation(sqtmp[:, 0, :], xh[:, i, :], ACT.Square, accum_out=st[:, i:i + 1]).then_inc(h_sq, 1)
                act_e.wait_ge(h_ms, i + 1)
                act_e.activation(st[:, 16 + i:17 + i], st[:, 8 + i:9 + i], ACT.Sqrt).then_inc(h_root, 1)
                for m in range(2):
                    act_e.wait_ge(xt_done, 2 * i + m + 1)
                    if i >= 2:
                        act_e.wait_ge(lg_done, i - 1)
                    act_e.activation(xrT[i % 2][:, 4 * m:4 * m + 4, :],
                                     ps[:, 6, :].rearrange("p (a b) -> p a b", a=4), ACT.Copy).then_inc(xt_out, 1)
            act_e.wait_ge(ex_in, 1)
            act_e.activation(ex[:, :, :], ex[:, :, :], ACT.Exp).then_inc(ex_done, 1)
            for i in range(2):
                act_e.wait_ge(gt_done, 4 * i + 4)
                act_e.wait_ge(padded, 2)
                act_e.activation(gatesT[0:E, i * HALF:(i + 1) * HALF], ps[0:E, i, :], ACT.Copy).then_inc(gt_out, 1)

            def take_xhi(n, g):
                act_e.wait_ge(xgt_done, n)
                act_e.activation(xT_hi[g][:, :, :], ps[:, 4 + 2 * g:6 + 2 * g, :].rearrange("p m (a b) -> p (m a) b", a=4),
                                 ACT.Copy).then_inc(xhi_ready, 1)

            act_e.wait_ge(op_done, 6 * NT)
            act_e.wait_ge(w_used, SPLIT)
            for s in range(LEAD):
                act_e.wait_ge(slot_in[s], 16)
                act_e.activation(w_hi[s][:, :, :], slot(s), ACT.Copy).then_inc(hi_ready, 1)
            act_e.wait_ge(ttab_ready, 1)
            for g in range(2):
                take_xhi(g + 1, g)
            act_e.wait_ge(init_out, 16 * NT)
            total = act_e.value_load(ttab[0:1, TALL:TALL + 1], min_val=1, max_val=NPASS)
            with act_e.Fori(0, total) as p:
                two = act_e.value_load(ttab[0:1, bass.ds(p + TTWO, 1)], min_val=0, max_val=1)
                dbl = act_e.value_load(ttab[0:1, bass.ds(p + TDBL, 1)], min_val=0, max_val=NPASS)
                p12 = act_e.snap(p * NSLOT)
                p32 = act_e.snap(p * 32)
                pieces = (act_e.snap(p * 4), act_e.snap(dbl * 4))
                x2 = act_e.snap(p * 2 + 2)

                def split_hi(s):
                    act_e.wait_ge(slot_in[s % RAW], p32 + 16 * (s // RAW + 1))
                    act_e.wait_ge(w_used, p12 + (s + 1))
                    act_e.activation(w_hi[s % SPLIT][:, :, :], slot(s), ACT.Copy).then_inc(hi_ready, 1)

                def body(groups):
                    def sigmoid(j):
                        for g in groups:
                            act_e.wait_ge(glu_ready[g], pieces[g] + (j + 1))
                            if j >= 2:
                                act_e.wait_ge(act_ready[g], pieces[g] + (j - 1))
                            act_e.activation(sig[:, g, j % 2, :], glu[:, g, j % 2, :], ACT.Sigmoid,
                                             scale=ALPHA).then_inc(sig_ready[g], 1)

                    def take_ahi(j):
                        for g in groups:
                            act_e.wait_ge(at_done[g], pieces[g] + (j + 1))
                            act_e.activation(actT_hi[g][:, 2 * j:2 * j + 2, :],
                                             ps[:, 7 - g, 0:256].rearrange("p (a b) -> p a b", a=2),
                                             ACT.Copy).then_inc(ahi_ready[g], 1)

                    split_hi(3)
                    split_hi(4)
                    for j in range(4):
                        split_hi(2 * j + 5)
                        sigmoid(j)
                        if j == 3:
                            take_xhi(x2 + 1, 0)
                        if j:
                            take_ahi(j - 1)
                        split_hi(2 * j + 6)
                    take_ahi(3)
                    split_hi(13)
                    split_hi(14)
                    take_xhi(x2 + 2, 1)

                with act_e.If(two > 0):
                    body((0, 1))
                with act_e.Else():
                    body((0,))

        @block.tensor
        def _(pe):
            pe.wait_ge(pool_const, 1)
            pe.wait_ge(vec_in, 16 * NVEC)
            pe.transpose(ps[:, 0, 0:NCOL], vrow[:, :], ident[0:NCOL, 0:NCOL]).then_inc(vec_ps, 1)
            tb = [0]

            def bank_of_transposes():
                n = tb[0]
                tb[0] += 1
                if n >= 4:
                    pe.wait_ge(tr_out, n - 3)
                return 4 + n % 4

            pe.wait_ge(scaled, 1)
            for k in range(0, KD, 2):
                b = bank_of_transposes()
                for kk in range(2):
                    for t in range(2):
                        m = pe.transpose(ps[:, b, kk * MEM + t * P:kk * MEM + (t + 1) * P],
                                         ms[:, t, (k + kk) * P:(k + kk + 1) * P], ident[:, :])
                m.then_inc(tr_done, 1)

            def x_transposes(h):
                pe.wait_ge(scaled, 2 + h)
                for k in range(KD):
                    b = bank_of_transposes()
                    for t in range(4):
                        m = pe.transpose(ps[:, b, t * P:(t + 1) * P], xs[:, t, k * P:(k + 1) * P], ident[:, :])
                    m.then_inc(tr_done, 1)

            x_transposes(0)
            pe.wait_ge(w_mem_in, 16)
            pe.wait_ge(tr_out, 4)
            pe.wait_ge(vec_ready, 1)
            for u in range(4):
                for k in range(KD):
                    if u < 2:
                        m = pe.matmul(ps[:, u, 0:MEM], w_mem[:, k, u * P:(u + 1) * P], memT_v[:, k, :],
                                      start=k == 0, stop=k == KD - 1)
                    else:
                        m = pe.matmul(ps[:, u, 0:MEM], memT_v[:, k, (u - 2) * P:(u - 1) * P], w_mem[:, k, MEM:2 * MEM],
                                      start=k == 0, stop=k == KD - 1)
                m.then_inc(mkv_done, 1)
            x_transposes(1)

            def unit(i):
                h, c = units[i]
                if i < 4:
                    pe.wait_ge(mkv_out, i + 1)
                else:
                    pe.wait_ge(in_out, i - 3)
                pe.wait_ge(tr_out, 4 + 8 * (h + 1))
                if c < 6:
                    pe.wait_ge(wA_in[c // 3], 16)
                    w = wA[:, :, c * P:(c + 1) * P]
                else:
                    pe.wait_ge(wB_in[{K: 0, V: 0, Q: 1, Q + 1: 1, Q + 2: 1}.get(c, 2)], 16)
                    w = wB[:, :, (c - 6) * P:(c - 5) * P]
                if c == V:
                    for t in range(4):
                        for k in range(KD):
                            m = pe.matmul(ps[:, i % 4, t * P:(t + 1) * P], xnT[:, k, (4 * h + t) * P:(4 * h + t + 1) * P],
                                          w[:, k, :], start=k == 0, stop=k == KD - 1)
                else:
                    for k in range(KD):
                        m = pe.matmul(ps[:, i % 4, :], w[:, k, :], xnT[:, k, h * HALF:(h + 1) * HALF],
                                      start=k == 0, stop=k == KD - 1)
                m.then_inc(in_done, 1)

            def gate_products(c):
                pe.wait_ge(conv_done, c + 1)
                pe.wait_ge(gw_in, 64)
                if c == 0:
                    pe.wait_ge(tr_out, 20)
                else:
                    pe.wait_ge(gate_act, 4 * c)
                for g in range(2):
                    for h in range(2):
                        pe.matmul(ps[:, 4 + 2 * g + h, :], gate_w[:, g, c, :], lru_tmp[:, 0, h * HALF:(h + 1) * HALF],
                                  start=True, stop=True).then_inc(gate_mm, 1)

            for i in range(12):
                unit(i)
            for c in range(LT):
                for i in range(12 + 5 * c, min(12 + 5 * c + 5, len(units))):
                    unit(i)
                gate_products(c)
            pe.wait_ge(pool_const, NPOOLC)
            pe.wait_ge(gate_act, 4 * LT)
            for n, (t, w, g) in enumerate(normt):
                pe.wait_ge(nsq, n + 1)
                for h in range(w // HALF):
                    m = pe.matmul(ps[0:NH, 4 + h, :], headcol[:, NH - 2 * n:2 * NH - 2 * n],
                                  sqtmp[:, n % 2, h * HALF:(h + 1) * HALF],
                                  start=n == 0, stop=n == len(normt) - 1)
                m.then_inc(nss, 1)
            for u, (h, n) in enumerate(norm_units):
                pe.wait_ge(rroot_ready, h + 1)
                if u >= 4:
                    pe.wait_ge(normed, u - 3)
                pe.matmul(ps[:, 4 + u % 4, :], headrow[:, 2 * n:2 * n + 2, :].rearrange("p a b -> p (a b)"),
                          rroot[:, h * HALF:(h + 1) * HALF], start=True, stop=True).then_inc(spread, 1)
            pe.wait_ge(normed, len(norm_units))
            pe.wait_ge(kz_in, 64)

            def scores(j):
                kind, b = items[j]
                for k, hs in enumerate(score_banks(kind)):
                    u = scb[j] + k
                    if u >= 4:
                        pe.wait_ge(sc_out, u - 3)
                    for n, h in enumerate(hs):
                        lo = P if kind == "swa" and b == 0 else 0
                        if kind == "swa":
                            qs = uT[:, Q + h // 2, b * P:(b + 1) * P]
                            keys = kz[h // 3][h % 2][:, (b - 1) * P + lo:(b + 1) * P]
                        else:
                            qs = uT[:, QM + h // 2, b * P:(b + 1) * P]
                            keys = kmz[:, h, :]
                        m = pe.matmul(ps[:, u % 4, n * 256 + lo:n * 256 + 256], qs, keys, start=True, stop=True)
                    m.then_inc(sc_done, 1)

            def transpose_probs(j):
                kind, b = items[j]
                for k in range(heads(kind) // 2):
                    pe.wait_ge(exp_done, hc[j] + 2 * k + 2)
                    if k % 2 == 0:
                        if ptac[j] + k // 2:
                            pe.wait_ge(pt_act, ptac[j] + k // 2)
                    elif j:
                        pe.wait_ge(pt_dve, j)
                    for a in range(4):
                        h, part = 2 * k + a // 2, a % 2
                        m = pe.transpose(ps[:, 4 + k % 2, a * P:(a + 1) * P], scores_sb[:, j % 3, h, part * P:(part + 1) * P],
                                         ident[:, :])
                    m.then_inc(pt_done, 1)

            def values(j):
                kind, b = items[j]
                pe.wait_ge(pt_act, ptac[j + 1])
                pe.wait_ge(pt_dve, j + 1)
                if j:
                    pe.wait_ge(o_ready, j)
                for h in range(heads(kind)):
                    parts = [1] if kind == "swa" and b == 0 else [0, 1]
                    for part in parts:
                        if kind == "swa":
                            v = uT[:, V, (b - 1 + part) * P + (h // 3) * DH:(b - 1 + part) * P + (h // 3 + 1) * DH]
                        else:
                            v = vm[:, part, h * DH:(h + 1) * DH]
                        m = pe.matmul(ps[:, 6, h * DH:(h + 1) * DH], probsT[:, 2 * h + part, :], v,
                                      start=part == parts[0], stop=part == 1)
                m.then_inc(pv_done, 1)

            def transpose_o(j):
                kind, b = items[j]
                pe.wait_ge(o_ready, j + 1)
                if j:
                    pe.wait_ge(yt_out, ytc[j])
                for t in range(heads(kind) // 2):
                    m = pe.transpose(ps[:, 7, t * P:(t + 1) * P], o_sb[:, j % 2, t * P:(t + 1) * P], ident[:, :])
                m.then_inc(yt_done, 1)

            scores(0)
            scores(1)
            for j in range(len(items)):
                transpose_probs(j)
                if j + 2 < len(items):
                    scores(j + 2)
                values(j)
                if j:
                    transpose_o(j - 1)
            transpose_o(len(items) - 1)
            pe.wait_ge(lru_sq, LT)
            for i in range(NT):
                for c in range(LT):
                    m = pe.matmul(ps[:, 0, i:i + 1], lru_tmp[:, 3 + c, i * P:(i + 1) * P], ones[:, 0:1],
                                  start=c == 0, stop=c == LT - 1)
            m.then_inc(lru_ss, 1)

            groups = ([LRU, LRU + 1, LRU + 2], [Q, Q + 1, Q + 2], [QM, QM + 1])
            pe.wait_ge(wout_in, 16)
            pe.wait_ge(lru_gained, LT)
            pe.wait_ge(grp_ms, 1)
            pe.wait_ge(yt_out, ytc[-1])
            pe.wait_ge(rt_in, 16 * NRT)

            def project(i):
                kk = 0
                for g, tiles in enumerate(groups):
                    for half in range(2):
                        if i:
                            pe.wait_ge(op_out, 6 * (i - 1) + 2 * g + half + 1)
                        for n, c in enumerate(tiles):
                            m = pe.matmul(ps[:, 2 * g + half, :], uT[:, c, i * P:(i + 1) * P],
                                          w_out_sb[:, kk + n, half * HALF:(half + 1) * HALF],
                                          start=n == 0, stop=n == len(tiles) - 1)
                        m.then_inc(op_done, 1)
                    kk += len(tiles)

            def route(i):
                pe.wait_ge(xr_ready, i + 1)
                for m2 in range(2):
                    if 2 * i + m2:
                        pe.wait_ge(xt_out, 2 * i + m2)
                    for a in range(4):
                        m = pe.transpose(ps[:, 6, a * P:(a + 1) * P], xrow[i % 2][:, (4 * m2 + a) * P:(4 * m2 + a + 1) * P],
                                         ident[:, :])
                    m.then_inc(xt_done, 1)
                pe.wait_ge(xt_out, 2 * i + 2)
                if i:
                    pe.wait_ge(lg_out, i)
                for k in range(KD):
                    m = pe.matmul(ps[:, 7, 0:E], xrT[i % 2][:, k, :], w_rt[:, k, :], start=k == 0, stop=k == KD - 1)
                m.then_inc(lg_done, 1)

            for i in range(NT + 1):
                if i < NT:
                    project(i)
                if i >= 1:
                    route(i - 1)

            def token_ids(n):
                pe.wait_ge(onehot_ready, n)
                for g in range(2):
                    for i in range(NT):
                        m = pe.matmul(ps[:, 6, g:g + 1], onehot[:, i, g * P:(g + 1) * P], tokid[:, i:i + 1],
                                      start=i == 0, stop=i == NT - 1)
                m.then_inc(ids_done, 1)

            pe.wait_ge(mask_ready, 1)
            pe.wait_ge(op_out, 6 * NT)
            for i in range(NT):
                for j in range(i + 1):
                    m = pe.matmul(ps[:, 2, i * E:(i + 1) * E], onesb[:, :] if j < i else tri[:, :], maskb[:, j, :],
                                  start=j == 0, stop=j == i)
            for j in range(NT):
                m = pe.matmul(ps[:, 3, 0:E], onesb[:, :], maskb[:, j, :], start=j == 0, stop=j == NT - 1)
            m.then_inc(pos_done, 1)
            pe.wait_ge(ptab_ready, 1)
            for a in range(3):
                m = pe.transpose(ps[0:1, 4, a * P:(a + 1) * P], ptab[:, a:a + 1], ident[:, :])
            m.then_inc(ttab_ps, 1)
            pe.wait_ge(gates_ready, 1)
            for i in range(NT):
                pe.transpose(ps[0:E, i // 4, (i % 4) * P:(i % 4 + 1) * P], gates[:, i, :], ident[:, :]).then_inc(gt_done, 1)
            token_ids(1)
            pe.wait_ge(gt_out, 2)
            pe.wait_ge(b2_in, 16)
            for i in range(NT):
                for half in range(2):
                    u = 2 * i + half
                    if u >= 2:
                        pe.wait_ge(init_ready, u - 1)
                    pe.matmul(ps[:, 2 + u % 2, :], gatesT[:, i * P:(i + 1) * P], b2_sb[:, half * HALF:(half + 1) * HALF],
                              start=True, stop=True).then_inc(init_mm, 1)

            def transpose_x(g):
                for k in range(KD):
                    m = pe.transpose(ps[:, 4 + 2 * g + k // 4, k % 4 * P:(k % 4 + 1) * P], xg[:, g, k * P:(k + 1) * P],
                                     ident[:, :])
                m.then_inc(xgt_done, 1)

            def three(acc, hi, lo, whi, wlo, first, last):
                pe.matmul(acc, hi, whi, start=first, stop=False)
                pe.matmul(acc, hi, wlo, start=False, stop=False)
                return pe.matmul(acc, lo, whi, start=False, stop=last)

            pe.wait_ge(idx_ready, 1)
            pe.wait_ge(xg_in, 32)
            for g in range(2):
                transpose_x(g)
            total = pe.value_load(ttab[0:1, TALL:TALL + 1], min_val=1, max_val=NPASS)
            with pe.Fori(0, total) as p:
                two = pe.value_load(ttab[0:1, bass.ds(p + TTWO, 1)], min_val=0, max_val=1)
                dbl = pe.value_load(ttab[0:1, bass.ds(p + TDBL, 1)], min_val=0, max_val=NPASS)
                p_dve, p_pool = pe.snap(p * (NSLOT - len(BY_POOL))), pe.snap(p * len(BY_POOL))

                def wait_split(s):
                    if s in BY_POOL:
                        pe.wait_ge(lo_pool, p_pool + split_before(s, True))
                    else:
                        pe.wait_ge(lo_ready, p_dve + split_before(s, False))

                pieces = (pe.snap(p * 4), pe.snap(dbl * 4))
                halves = (pe.snap(p * 2), pe.snap(dbl * 2))
                x2 = pe.snap(p * 2)
                x32 = pe.snap(p * 32 + 64)

                def body(groups):
                    def transpose_act(j):
                        for g in groups:
                            pe.wait_ge(act_ready[g], pieces[g] + (j + 1))
                            if j:
                                pe.wait_ge(alo_ready[g], pieces[g] + j)
                            elif g:
                                pe.wait_ge(idx_ready, p + 2)
                            for a in range(2):
                                m = pe.transpose(ps[:, 7 - g, a * P:(a + 1) * P],
                                                 act[:, g, j % 2, a * P:(a + 1) * P], ident[:, :])
                            m.then_inc(at_done[g], 1)

                    def up(s):
                        j, kh = s // 2, s % 2
                        wait_split(s)
                        for g in groups:
                            if kh == 0:
                                if j == 0:
                                    pe.wait_ge(combined[g], halves[g] + 1)
                                pe.wait_ge(h_free[g], pieces[g] + (j + 1))
                                if j == 0:
                                    pe.wait_ge(xlo_ready, x2 + (g + 1))
                            for k in range(4):
                                kk = 4 * kh + k
                                m = three(ps[:, 2 * (j % 2) + g, :], xT_hi[g][:, kk, :], xT_lo[g][:, kk, :],
                                          w_hi[s % SPLIT][:, k, :], w_lo[s % SPLIT][:, k, :], kk == 0, kk == KD - 1)
                        m.then_inc(w_used, 1)

                    def down(s, ks):
                        kh, b = (s - 8) // 2, s % 2
                        if ks[0] == 0:
                            wait_split(s)
                        for g in groups:
                            if kh == 0 and b == 0:
                                pe.wait_ge(h_free[g], pieces[g] + 5)
                            if kh == 0 and b == 1:
                                pe.wait_ge(xlo_ready, x2 + 3)
                            for k in ks:
                                kk = 4 * kh + k
                                if k % 2 == 0:
                                    pe.wait_ge(alo_ready[g], pieces[g] + (kk // 2 + 1))
                                m = three(ps[:, 4 * b + g, :], actT_hi[g][:, kk, :], actT_lo[g][:, kk, :],
                                          w_hi[s % SPLIT][:, k, :], w_lo[s % SPLIT][:, k, :], kk == 0, kk == KD - 1)
                        if ks[-1] == 3:
                            m.then_inc(w_used, 1)

                    up(0)
                    pe.wait_ge(xlo_ready, x2 + 2)
                    token_ids(p + 2)
                    for s in range(1, 8):
                        up(s)
                        if s in (4, 6):
                            transpose_act((s - 4) // 2)
                    pe.wait_ge(xg_in, x32)
                    for g in range(2):
                        pe.wait_ge(combined[g], halves[g] + 2)
                    transpose_x(0)
                    down(8, range(0, 4))
                    transpose_act(2)
                    down(9, range(0, 4))
                    transpose_act(3)
                    down(10, range(0, 4))
                    pe.wait_ge(idx_ready, p + 2)
                    for g in groups:
                        pe.wait_ge(alo_ready[g], pieces[g] + 4)
                    transpose_x(1)
                    down(11, range(0, 4))

                with pe.If(two > 0):
                    body((0, 1))
                with pe.Else():
                    body((0,))

        @block.vector
        def _(dve):
            chain = [0]

            def link(ins):
                chain[0] += 1
                ins.then_inc(dve_step, 1)
                dve.wait_ge(dve_step, chain[0])

            dve.wait_ge(vec_ps, 1)
            link(dve.tensor_copy(vecs[:, 0:NCOL], ps[:, 0, 0:NCOL]))
            dve.memset(vecs[:, C_EPS:C_EPS + 1], EPS)
            lam = col(C_LAM, LT)
            L = [lamt[:, i, :] for i in range(6)]
            link(dve.tensor_scalar(L[0], lam, -1.0, None, ALU.mult))
            dve.tensor_tensor(L[1], L[0], lam, ALU.min).then_inc(lam_in, 1)
            dve.memset(credit[:, 3:4], 0.0).then_inc(vec_ready, 1)
            for n, (a, b) in enumerate(((0, 2), (2, 6), (6, 10))):
                dve.wait_ge(sq_sum, b)
                dve.tensor_scalar(st[:, 16 + a:16 + b], st[:, a:b], 1.0 / D, EPS, ALU.mult, ALU.add).then_inc(ms_ready, 1)
                dve.wait_ge(rt_ready, n + 1)
                link(dve.reciprocal(st[:, 16 + a:16 + b], st[:, 32 + a:32 + b]))
                if n == 2:
                    dve.wait_ge(tr_done, 12)
                for t in range(a, b):
                    if t < 2:
                        m = dve.tensor_scalar(ms[:, t, :], mem_sb[:, t, :], st[:, 16 + t:17 + t], None, ALU.mult)
                    else:
                        m = dve.tensor_scalar(xs[:, (t - 2) % 4, :], xh[:, t - 2, :], st[:, 16 + t:17 + t], None, ALU.mult)
                m.then_inc(scaled, 1)
                if n == 0:
                    for k in range(0, KD, 2):
                        dve.wait_ge(tr_done, k // 2 + 1)
                        for kk in range(2):
                            m = dve.tensor_scalar(memT_v[:, k + kk, :], ps[:, 4 + (k // 2) % 4, kk * MEM:(kk + 1) * MEM],
                                                  col(C_GMEM + k + kk), None, ALU.mult)
                        m.then_inc(tr_out, 1)
                else:
                    h = n - 1
                    for k in range(KD):
                        u = 4 + 8 * h + k
                        dve.wait_ge(tr_done, u + 1)
                        dve.tensor_scalar(xnT[:, k, h * HALF:(h + 1) * HALF], ps[:, 4 + u % 4, :], col(C_GMIX + k), None,
                                          ALU.mult).then_inc(tr_out, 1)
            dve.wait_ge(lam_exp, 1)
            link(dve.tensor_scalar(L[2], L[1], 2.0, None, ALU.add))
            link(dve.reciprocal(L[2], L[2]))
            link(dve.tensor_tensor(L[2], L[1], L[2], ALU.mult))
            link(dve.tensor_tensor(L[3], L[2], L[2], ALU.mult))
            link(dve.tensor_scalar(L[4], L[3], 1.0 / 17, 1.0 / 15, ALU.mult, ALU.add))
            for d in (13, 11, 9, 7, 5, 3, 1):
                link(dve.tensor_tensor(L[4], L[4], L[3], ALU.mult))
                link(dve.tensor_scalar(L[4], L[4], 1.0 / d, None, ALU.add))
            link(dve.scalar_tensor_tensor(out=L[4], in0=L[4], scalar=2.0, in1=L[2], op0=ALU.mult, op1=ALU.mult))
            link(dve.scalar_tensor_tensor(out=L[4], in0=L[0], scalar=0.0, in1=L[4], op0=ALU.max, op1=ALU.add))
            dve.tensor_scalar(col(C_NSP8, LT), L[4], -8.0, None, ALU.mult)
            dve.tensor_scalar(col(C_SP8, LT), L[4], 8.0, None, ALU.mult).then_inc(dve_const, 1)

            for c in range(LT):
                u, xc = uT[:, LRU + c, :], lru_tmp[:, 0, :]
                dve.wait_ge(in_out, upos[(1, LRU + c)] + 1)
                if c == 0:
                    dve.wait_ge(in_done, 12)
                link(dve.tensor_scalar(xc, u, col(C_CONVW + 9 + c), col(C_CONVB + c), ALU.mult, ALU.add))
                for back in (1, 2, 3):
                    m = dve.scalar_tensor_tensor(out=xc[:, back:S], in0=u[:, 0:S - back], scalar=col(C_CONVW + 3 * (3 - back) + c),
                                                 in1=xc[:, back:S], op0=ALU.mult, op1=ALU.add)
                    if back < 3:
                        link(m)
                m.then_inc(conv_done, 1)
                t, a, w = lru_tmp[:, 3, :], lru_tmp[:, 4, :], lru_tmp[:, 5, :]
                dve.wait_ge(ab_ready, 2 * c + 2)
                link(dve.tensor_tensor(w, a, a, ALU.mult))
                dve.scalar_tensor_tensor(out=t, in0=w, scalar=1.0, in1=t, op0=ALU.add, op1=ALU.mult).then_inc(frac_ready, 1)
                ix = lru_tmp[:, 2, :]
                dve.wait_ge(gate_act, 4 * c + 4)
                dve.wait_ge(conv_done, c + 1)
                link(dve.tensor_tensor(ix, ix, xc, ALU.mult))
                dve.wait_ge(root_ready, c + 1)
                link(dve.tensor_tensor(ix, ix, t, ALU.mult))
                dve.wait_ge(ab_ready, 2 * c + 2)
                dve.tensor_tensor_scan(u, lru_tmp[:, 4, :], ix, 0.0, ALU.mult, ALU.add).then_inc(ylru, 1)
                dve.wait_ge(ylru, 2 * c + 1)
                dve.wait_ge(gelu_done, c + 1)
                dve.tensor_tensor(u, u, uT[:, GATE + c, :], ALU.mult).then_inc(ylru, 1)

            dve.wait_ge(nroot, 2)
            for h in range(2):
                dve.reciprocal(rroot[0:NH, h * HALF:(h + 1) * HALF],
                               rroot[0:NH, h * HALF:(h + 1) * HALF]).then_inc(rroot_ready, 1)
            for u, (h, n) in enumerate(norm_units):
                t, w, g = normt[n]
                dve.wait_ge(spread, u + 1)
                if n == 1:
                    dve.wait_ge(kz_zero, 5)
                    for o in (0, 1):
                        r = slice(o * DH, (o + 1) * DH)
                        m = dve.scalar_tensor_tensor(out=kmz[r, o::2, :], in0=km[r, :, :], scalar=col(g)[r],
                                                     in1=ps[r, 4 + u % 4, :].rearrange("p (a b) -> p a b", a=2),
                                                     op0=ALU.mult, op1=ALU.mult)
                    m.then_inc(normed, 1)
                else:
                    th = t[:, h * HALF:(h + 1) * HALF]
                    dve.scalar_tensor_tensor(out=th, in0=th, scalar=col(g), in1=ps[:, 4 + u % 4, :],
                                             op0=ALU.mult, op1=ALU.mult).then_inc(normed, 1)

            scale = DH ** -0.5
            dve.wait_ge(rt_in, 16 * NRT)
            dve.wait_ge(pool_const, NPOOLC)
            link(dve.tensor_scalar(st[:, 88:94], sinkb[:, :], -1.0, None, ALU.mult))

            def softmax_in(j):
                kind, b = items[j]
                nh = heads(kind)
                sc = scores_sb[:, j % 3, 0:nh, :]
                for k, hs in enumerate(score_banks(kind)):
                    n = len(hs)
                    dve.wait_ge(sc_done, scb[j] + k + 1)
                    if j == 0 and k == 0:
                        dve.wait_ge(in_done, len(units))
                    if j >= 3 and k == 0:
                        dve.wait_ge(pt_done, ytc[j - 2])
                    src = ps[:, (scb[j] + k) % 4, :].rearrange("p (h k) -> p h k", h=n)
                    dst = scores_sb[:, j % 3, hs[0]:hs[-1] + 1, :]
                    if kind == "swa":
                        if b == 0:
                            dve.tensor_copy(dst[:, :, 0:P], band[:, 1:2, 0:P].to_broadcast([P, n, P]))
                            src, dst, mk = src[:, :, P:2 * P], dst[:, :, P:2 * P], band[:, 1:2, P:2 * P].to_broadcast([P, n, P])
                        else:
                            mk = band[:, 0:1, :].to_broadcast([P, n, 2 * P])
                        dve.scalar_tensor_tensor(out=dst, in0=src, scalar=scale, in1=mk,
                                                 op0=ALU.mult, op1=ALU.add).then_inc(sc_out, 1)
                    else:
                        dve.tensor_scalar(dst, src, scale, None, ALU.mult).then_inc(sc_out, 1)
                dve.wait_ge(sc_out, scb[j + 1])
                mx = nmx[j % 3][:, 0:nh]
                link(dve.tensor_reduce(mx, sc, AX_X, ALU.max))
                if kind == "swa":
                    dve.scalar_tensor_tensor(out=mx, in0=mx, scalar=-1.0, in1=st[:, 88:94],
                                             op0=ALU.mult, op1=ALU.min).then_inc(nmx_ready, 1)
                    dve.wait_ge(nmx_ready, j + 1)
                    dve.tensor_tensor(sinkx[b % 2], mx, sinkb[:, :], ALU.add).then_inc(sink_in, 1)
                else:
                    dve.tensor_scalar(mx, mx, -1.0, None, ALU.mult).then_inc(nmx_ready, 1)

            def softmax_out(j):
                kind, b = items[j]
                nh = heads(kind)
                sums = row_sums[j % 3][:, 0:nh]
                dve.wait_ge(exp_done, hc[j + 1])
                if kind == "swa":
                    dve.wait_ge(sink_exp, b + 1)
                    link(dve.tensor_tensor(sums, sums, sinkx[b % 2], ALU.add))
                link(dve.reciprocal(sums, sums))
                dve.wait_ge(pt_done, ytc[j] + 2)
                if j:
                    dve.wait_ge(pv_done, j)
                dve.tensor_copy(probsT[:, 4:8, :], ps[:, 5, :].rearrange("p (a b) -> p a b", a=4)).then_inc(pt_dve, 1)

            def normalise(j):
                kind, b = items[j]
                nh = heads(kind)
                sums = row_sums[j % 3][:, 0:nh]
                dve.wait_ge(pv_done, j + 1)
                if j >= 2:
                    dve.wait_ge(o_ss, j - 1)
                    dve.wait_ge(yt_done, j - 1)
                dve.tensor_tensor(o_sb[:, j % 2, 0:nh * DH].rearrange("p (h d) -> p h d", h=nh),
                                  ps[:, 6, 0:nh * DH].rearrange("p (h d) -> p h d", h=nh),
                                  sums.rearrange("p (h a) -> p h a", a=1).to_broadcast([P, nh, DH]),
                                  ALU.mult).then_inc(o_ready, 1)

            def take_y(j):
                kind, b = items[j]
                dve.wait_ge(yt_done, j + 1)
                base, g = (Q, C_GOS) if kind == "swa" else (QM, C_GOM)
                for t in range(heads(kind) // 2):
                    dve.tensor_scalar(uT[:, base + t, b * P:(b + 1) * P], ps[:, 7, t * P:(t + 1) * P], col(g + t), None,
                                      ALU.mult).then_inc(yt_out, 1)

            softmax_in(0)
            softmax_in(1)
            for j in range(len(items)):
                if j:
                    normalise(j - 1)
                softmax_out(j)
                if j + 2 < len(items):
                    softmax_in(j + 2)
                if j >= 2:
                    take_y(j - 2)
            normalise(len(items) - 1)
            for j in (-2, -1):
                take_y(len(items) + j)
            dve.wait_ge(o_ss, len(items))
            dve.wait_ge(lru_ss, 1)
            link(dve.tensor_scalar(grp[:, 0:8], ps[:, 0, 0:NT], 1.0 / DL, EPS, ALU.mult, ALU.add))
            sso = st[:, 96:112].rearrange("p (b two) -> p two b", two=2)
            link(dve.tensor_scalar(grp[:, 8:16], sso[:, 0, :], 1.0 / DL, EPS, ALU.mult, ALU.add))
            dve.tensor_scalar(grp[:, 16:24], sso[:, 1, :], 1.0 / (NM * DH), EPS, ALU.mult, ALU.add).then_inc(grp_ms, 1)
            dve.wait_ge(grp_root, 1)
            link(dve.reciprocal(grp[:, 0:24], grp[:, 0:24]))

            def residual(i):
                for g in range(3):
                    for half in range(2):
                        n = 6 * i + 2 * g + half
                        dve.wait_ge(op_done, n + 1)
                        if g:
                            dve.wait_ge(op_out, n - 1)
                        hh = xh[:, i, half * HALF:(half + 1) * HALF]
                        dve.scalar_tensor_tensor(out=hh, in0=ps[:, 2 * g + half, :], scalar=grp[:, 8 * g + i:8 * g + i + 1],
                                                 in1=hh, op0=ALU.mult, op1=ALU.add).then_inc(op_out, 1)

            def ffn_norm(i):
                dve.wait_ge(h_sq, i + 1)
                dve.tensor_scalar(st[:, 8 + i:9 + i], st[:, i:i + 1], 1.0 / D, EPS, ALU.mult, ALU.add).then_inc(h_ms, 1)
                dve.wait_ge(h_root, i + 1)
                link(dve.reciprocal(st[:, 24 + i:25 + i], st[:, 16 + i:17 + i]))
                if i >= 2:
                    dve.wait_ge(xt_done, 2 * (i - 2) + 2)
                    dve.wait_ge(xrow_out[i % 2], 16 * (i // 2))
                dve.scalar_tensor_tensor(out=xrow[i % 2], in0=xh[:, i, :], scalar=st[:, 24 + i:25 + i], in1=gbc,
                                         op0=ALU.mult, op1=ALU.mult).then_inc(xr_ready, 1)

            def take_logits(i):
                dve.wait_ge(lg_done, i + 1)
                dve.tensor_tensor(lg[:, i, :], ps[:, 7, 0:E], b_rt[:, :], ALU.add).then_inc(lg_out, 1)

            dve.wait_ge(gbc_in, 16)
            for i in range(NT + 1):
                if i < NT:
                    residual(i)
                    ffn_norm(i)
                if i >= 1:
                    take_logits(i - 1)
            dve.wait_ge(lg_out, NT)
            for i in range(NT):
                m = dve.max(top8[:, i, :], lg[:, i, :])
            link(m)
            for i in range(NT):
                m = dve.max_index(idx8[:, i, :], top8[:, i, :], lg[:, i, :])
            link(m)
            dve.tensor_tensor(ex[:, :, :], lg[:, :, :], top8[:, :, 0:1].to_broadcast([P, NT, E]),
                              ALU.subtract).then_inc(ex_in, 1)
            link(dve.tensor_copy(idxf[:, :, :], idx8[:, :, :]))
            ie = iota_e[:, :].rearrange("p (a e) -> p a e", a=1).to_broadcast([P, NT, E])
            link(dve.tensor_tensor(mask[:, :, :], ie, idxf[:, :, 0:1].to_broadcast([P, NT, E]), ALU.is_equal))
            for k in range(1, TOPK):
                link(dve.tensor_tensor(tmpe[:, :, :], ie, idxf[:, :, k:k + 1].to_broadcast([P, NT, E]), ALU.is_equal))
                link(dve.tensor_tensor(mask[:, :, :], mask[:, :, :], tmpe[:, :, :], ALU.add))
            dve.tensor_copy(maskb[:, :, :], mask[:, :, :]).then_inc(mask_ready, 1)
            dve.wait_ge(ex_done, 1)
            link(dve.tensor_tensor(gates[:, :, :], ex[:, :, :], mask[:, :, :], ALU.mult))
            link(dve.tensor_reduce(st[:, 0:NT], gates[:, :, :], AX_X, ALU.add))
            link(dve.reciprocal(st[:, 8:8 + NT], st[:, 0:NT]))
            dve.tensor_tensor(gates[:, :, :], gates[:, :, :],
                              st[:, 8:8 + NT].rearrange("p (t a) -> p t a", a=1).to_broadcast([P, NT, E]),
                              ALU.mult).then_inc(gates_ready, 1)
            dve.wait_ge(pos_done, 1)
            link(dve.scalar_tensor_tensor(out=posm[:, :, :], in0=ps[:, 2, 0:NT * E].rearrange("p (t e) -> p t e", t=NT),
                                          scalar=1.0, in1=mask[:, :, :], op0=ALU.add, op1=ALU.mult))
            link(dve.tensor_scalar(posm[:, :, :], posm[:, :, :], -1.0, None, ALU.add))
            link(dve.tensor_copy(cnt[:, :], ps[:, 3, 0:E]))
            link(dve.tensor_scalar(npass[:, :], cnt[:, :], 0.0, None, ALU.is_gt))
            for j in range(1, MAXPART):
                link(dve.scalar_tensor_tensor(out=npass[:, :], in0=cnt[:, :], scalar=float(j * PASS), in1=npass[:, :],
                                              op0=ALU.is_gt, op1=ALU.add))
            link(dve.tensor_scalar(npass[:, 0:1], npass[:, 0:1], 1.0, None, ALU.max))
            link(dve.tensor_tensor_scan(cum[:, :], npass[:, :], npass[:, :], 0.0, ALU.add, ALU.max))
            link(dve.tensor_scalar(tmpe[:, 0, :], cum[:, :], iota_p[:, 0:1], None, ALU.is_le))
            link(dve.tensor_tensor(tmpe[:, 1, :], tmpe[:, 0, :], cum[:, :], ALU.mult))
            link(dve.tensor_reduce(st[:, 16:17], tmpe[:, 0, :], AX_X, ALU.add))
            link(dve.tensor_reduce(st[:, 18:19], tmpe[:, 1, :], AX_X, ALU.max))
            link(dve.tensor_scalar(ptab[:, 0:1], st[:, 16:17], float(E - 1), None, ALU.min))
            link(dve.tensor_tensor(ptab[:, 1:2], iota_p[:, 0:1], st[:, 18:19], ALU.subtract))
            link(dve.tensor_scalar(ptab[:, 1:2], ptab[:, 1:2], float(MAXPART), None, ALU.min))
            link(dve.tensor_scalar(tmpe[:, 2, :], iota_e[:, :], ptab[:, 0:1], None, ALU.is_equal))
            link(dve.tensor_tensor(tmpe[:, 2, :], tmpe[:, 2, :], cnt[:, :], ALU.mult))
            link(dve.tensor_reduce(st[:, 19:20], tmpe[:, 2, :], AX_X, ALU.add))
            link(dve.scalar_tensor_tensor(out=st[:, 20:21], in0=ptab[:, 1:2], scalar=float(-PASS), in1=st[:, 19:20],
                                          op0=ALU.mult, op1=ALU.add))
            dve.tensor_scalar(ptab[:, 2:3], st[:, 20:21], float(P), None, ALU.is_gt).then_inc(ptab_ready, 1)
            link(dve.tensor_copy(ttab[0:1, TALL:TALL + 1], cum[0:1, E - 1:E]))
            dve.wait_ge(ttab_ps, 1)
            flags, upto = dblrow[:, 0:P], dblrow[:, P:2 * P]
            link(dve.tensor_copy(flags, ps[0:1, 4, 2 * P:3 * P]))
            link(dve.tensor_tensor_scan(upto, flags, flags, 0.0, ALU.add, ALU.max))
            link(dve.tensor_tensor(ttab[0:1, TDBL:TDBL + P], upto, flags, ALU.subtract))
            dve.tensor_copy(ttab[0:1, 0:3 * P], ps[0:1, 4, 0:3 * P]).then_inc(ttab_ready, 1)
            dve.wait_ge(ttab_ready, 1)
            dve.wait_ge(zeroed, 2)
            total = dve.value_load(ttab[0:1, TALL:TALL + 1], min_val=1, max_val=NPASS)

            def make_onehot(n):
                e = dve.value_load(ttab[0:1, bass.ds(n + TE, 1)], min_val=0, max_val=E - 1)
                part = dve.value_load(ttab[0:1, bass.ds(n + TPART, 1)], min_val=0, max_val=MAXPART)
                dve.tensor_tensor(onehot[:, :, :],
                                  iota_s[:, bass.ds(part * PASS, PASS)].rearrange("p (a s) -> p a s", a=1).to_broadcast([P, NT, PASS]),
                                  posm[:, :, bass.ds(e, 1)].to_broadcast([P, NT, PASS]), ALU.is_equal).then_inc(onehot_ready, 1)

            def make_idx(n):
                dve.wait_ge(ids_done, n)
                dve.tensor_scalar(pad[:, :], ps[:, 6, 0:2], 0.0, float(AHEAD_OOB), ALU.is_equal, ALU.mult).then_inc(moe_step, 1)
                dve.wait_ge(moe_step, n)
                dve.scalar_tensor_tensor(out=idx_next[:, :], in0=ps[:, 6, 0:2], scalar=-1.0, in1=pad[:, :],
                                         op0=ALU.add, op1=ALU.add).then_inc(idx_ready, 1)

            def minus_hi(lo, x, hi):
                return dve.tensor_tensor(lo, x, hi.bitcast(F32), ALU.subtract)

            def take_xlo(n, g):
                dve.wait_ge(xhi_ready, n)
                minus_hi(xT_lo[g][:, :, :], ps[:, 4 + 2 * g:6 + 2 * g, :].rearrange("p m (a b) -> p (m a) b", a=4),
                         xT_hi[g][:, :, :]).then_inc(xlo_ready, 1)

            for g in range(2):
                dve.memset(credit[:, g:g + 1], 0.0).then_inc(h_free[g], 2)
                dve.memset(credit[:, 2 + g:3 + g], 0.0).then_inc(combined[g], 2)
            dve.memset(credit[:, 4:5], 0.0).then_inc(w_used, SPLIT)
            dve.wait_ge(xr_ready, NT)
            make_onehot(0)
            make_idx(1)
            make_onehot(1)
            for u in range(2 * NT):
                i, half = u // 2, u % 2
                dve.wait_ge(init_mm, u + 1)
                hh = xh[:, i, half * HALF:(half + 1) * HALF]
                dve.tensor_tensor(hh, ps[:, 2 + u % 2, :], hh, ALU.add).then_inc(init_ready, 1)
            for s in range(LEAD):
                dve.wait_ge(hi_ready, s + 1)
                minus_hi(w_lo[s][:, :, :], slot(s), w_hi[s][:, :, :]).then_inc(lo_ready, 1)
            for g in range(2):
                take_xlo(g + 1, g)
            dve.wait_ge(init_out, 16 * NT)
            with dve.Fori(0, total) as p:
                e = dve.value_load(ttab[0:1, bass.ds(p + TE, 1)], min_val=0, max_val=E - 1)
                two = dve.value_load(ttab[0:1, bass.ds(p + TTWO, 1)], min_val=0, max_val=1)
                dbl = dve.value_load(ttab[0:1, bass.ds(p + TDBL, 1)], min_val=0, max_val=NPASS)
                p12 = dve.snap(p * NSLOT)
                pieces = (dve.snap(p * 4), dve.snap(dbl * 4))
                rows16 = (dve.snap(p * 16 + 16), dve.snap(dbl * 16 + 16))
                used = dve.snap(p * NSLOT + SPLIT)
                x2 = dve.snap(p * 2 + 2)
                dve.wait_ge(combined[0], p * 2 + 2)
                dve.wait_ge(combined[1], dbl * 2 + 2)
                dve.wait_ge(xg_in, p * 32 + 32)
                dve.tensor_copy(gate_cur[:, :].rearrange("p (g a) -> p g a", a=1),
                                xg[:, :, bass.ds(e + D, 1)]).then_inc(gate_copied, 1)

                def split_lo(s):
                    if s in BY_POOL:
                        return
                    dve.wait_ge(hi_ready, p12 + (s + 1))
                    minus_hi(w_lo[s % SPLIT][:, :, :], slot(s), w_hi[s % SPLIT][:, :, :]).then_inc(lo_ready, 1)

                def body(groups):
                    def add_bias(j):
                        dve.wait_ge(w_used, used + (2 * j + 2))
                        for g in groups:
                            n = pieces[g]
                            if len(groups) * j + g >= 2:
                                h2, j2 = (g, j - 1) if len(groups) == 2 else (0, j - 2)
                                dve.wait_ge(lin_ready[h2], pieces[h2] + (j2 + 1))
                            b = g if len(groups) == 2 else j % 2
                            hj = hb[:, b, :]
                            dve.tensor_tensor(hj, ps[:, 2 * (j % 2) + g, :], b1b[:, j * HALF:(j + 1) * HALF],
                                              ALU.add).then_inc(h_free[g], 1)
                            dve.wait_ge(h_free[g], n + (3 + j))
                            pair = hj.rearrange("p (n two) -> p two n", two=2)
                            if j >= 2:
                                dve.wait_ge(act_ready[g], n + (j - 1))
                            dve.tensor_scalar(glu[:, g, j % 2, :], pair[:, 0, :], LIMIT, None, ALU.min).then_inc(glu_ready[g], 1)
                            dve.tensor_scalar(lin[:, g, j % 2, :], pair[:, 1, :], LIMIT, -LIMIT, ALU.min,
                                              ALU.max).then_inc(lin_ready[g], 1)
                        for g in groups:
                            dve.wait_ge(lin_ready[g], pieces[g] + (j + 1))
                            dve.scalar_tensor_tensor(out=lin[:, g, j % 2, :], in0=lin[:, g, j % 2, :], scalar=1.0,
                                                     in1=glu[:, g, j % 2, :], op0=ALU.add, op1=ALU.mult).then_inc(lin_done[g], 1)

                    def times_sigmoid(j):
                        for g in groups:
                            dve.wait_ge(sig_ready[g], pieces[g] + (j + 1))
                            dve.wait_ge(lin_done[g], pieces[g] + (j + 1))
                            if j >= 2:
                                dve.wait_ge(at_done[g], pieces[g] + (j - 1))
                            dve.tensor_tensor(act[:, g, j % 2, :], lin[:, g, j % 2, :], sig[:, g, j % 2, :],
                                              ALU.mult).then_inc(act_ready[g], 1)

                    def take_alo(j):
                        for g in groups:
                            dve.wait_ge(ahi_ready[g], pieces[g] + (j + 1))
                            minus_hi(actT_lo[g][:, 2 * j:2 * j + 2, :],
                                     ps[:, 7 - g, 0:256].rearrange("p (a b) -> p a b", a=2),
                                     actT_hi[g][:, 2 * j:2 * j + 2, :]).then_inc(alo_ready[g], 1)

                    def combine(b):
                        dve.wait_ge(w_used, used + (11 + b))
                        for g in groups:
                            if b == 0:
                                dve.wait_ge(rows_in[g], rows16[g])
                            rb = rows[:, g, b * HALF:(b + 1) * HALF]
                            dve.scalar_tensor_tensor(out=rb, in0=ps[:, 4 * b + g, :], scalar=gate_cur[:, g:g + 1], in1=rb,
                                                     op0=ALU.mult, op1=ALU.add).then_inc(combined[g], 1)

                    split_lo(3)
                    dve.wait_ge(b1_in, p * 16 + 16)
                    split_lo(4)
                    for j in range(4):
                        add_bias(j)
                        if j == 0:
                            dve.wait_ge(idxcur_ready, p + 1)
                            make_idx(p + 2)
                        split_lo(2 * j + 5)
                        if j == 3:
                            take_xlo(x2 + 1, 0)
                        times_sigmoid(j)
                        if j:
                            take_alo(j - 1)
                        split_lo(2 * j + 6)
                        if j == 1:
                            make_onehot(p + 2)
                    take_alo(3)
                    split_lo(13)
                    combine(0)
                    split_lo(14)
                    take_xlo(x2 + 2, 1)
                    combine(1)

                with dve.If(two > 0):
                    body((0, 1))
                with dve.Else():
                    body((0,))
            dve.wait_ge(b1_in, total * 16 + 16)
            dve.memset(credit[:, 5:6], 0.0)
            for i in range(RAW):
                dve.wait_ge(slot_in[i], total * 32 + 16)
                dve.memset(credit[:, 8 + i:9 + i], 0.0)


_INS = ["x", "mem", "g_mix", "w_in", "conv_w", "conv_b", "lru_wa", "lru_ba", "lru_wx", "lru_bx", "lru_lambda",
        "q_norm_swa", "k_norm_swa", "swa_sinks", "g_mem", "w_mem_kv", "q_norm_mem", "k_norm_mem",
        "g_out_lru", "g_out_swa", "g_out_mem", "w_out", "g_ffn", "w_router", "b_router", "w1", "b1", "w2", "b2"]


def kernel(**inputs):
    import numpy as _np
    import concourse.bacc as _bacc
    from concourse.bass_utils import run_bass_kernel_spmd as _run

    nc = _bacc.Bacc("TRN2", target_bir_lowering=False, num_devices=1)
    arrays, args = {}, []
    for name in _INS:
        a = _np.ascontiguousarray(inputs[name])
        arrays[f"in_{name}"] = a
        args.append(nc.dram_tensor(f"in_{name}", a.shape, mybir.dt.from_np(a.dtype), kind="ExternalInput").ap())
    xrows = nc.dram_tensor("token_rows", (S, XW), F32, kind="Internal").ap()
    out = nc.dram_tensor("out", (1, S, D), F32, kind="ExternalOutput").ap()
    hymba_layer(nc, *args, xrows, out)
    r = _run(nc, [arrays], core_ids=[0])
    return r.results[0]["out"]
```
